# Optimizing a Trainium2 kernel written in Bass

```python
import math
import jax, jax.numpy as jnp
from jax import lax
import numpy as np

D_MODEL = 1024
BATCH = 1
SEQ = 256
DEPTH = 2
DEC_BATCH = 8
DEC_SEQ = 1
PAST_LEN = 2048
PAGE_SIZE = 128

GDN_HEAD_DIM = 128
GDN_HEADS = D_MODEL // GDN_HEAD_DIM
GDN_DK = GDN_HEAD_DIM
GDN_DV = GDN_HEAD_DIM
GDN_CONV = 4
GDN_CHUNK = 64
GDN_QK_W = GDN_HEADS * GDN_DK
GDN_V_W = GDN_HEADS * GDN_DV
GDN_CONV_CH = 2 * GDN_QK_W + GDN_V_W
GDN_IN_COLS = GDN_CONV_CH + GDN_V_W + 2 * GDN_HEADS
SC_WIDTH = 3
D_FF = ((8 * D_MODEL // 3) + 255) // 256 * 256
N_EXPERTS = 8
TOP_K = 2
D_FF_EXPERT = 7 * D_MODEL // 2
N_EVEN_LAYERS = (DEPTH + 1) // 2
N_ODD_LAYERS = DEPTH // 2
ALPHA = (2.0 * DEPTH) ** 0.25
BETA_INIT = (8.0 * DEPTH) ** -0.25
LN_EPS = 1e-5
NORM_EPS = 1e-6

kernel_name = 'hybrid_gdn_shortconv_moe_step'

def layer_norm(x, g, b):
    xf = x.astype(jnp.float32)
    mu = jnp.mean(xf, axis=-1, keepdims=True)
    var = jnp.mean(jnp.square(xf - mu), axis=-1, keepdims=True)
    y = (xf - mu) * lax.rsqrt(var + LN_EPS) * g.astype(jnp.float32) + b.astype(jnp.float32)
    return y.astype(x.dtype)

def l2_normalize(x):
    return x * lax.rsqrt(jnp.sum(jnp.square(x), axis=-1, keepdims=True) + NORM_EPS)

def causal_dwconv(u, buf, w):
    width, ch = w.shape
    full = jnp.concatenate([buf.astype(u.dtype), u], axis=1)
    out = lax.conv_general_dilated(full, w[:, None, :].astype(u.dtype), window_strides=(1,), padding='VALID',
                                   dimension_numbers=('NWC', 'WIO', 'NWC'), feature_group_count=ch)
    return out, full[:, full.shape[1] - (width - 1):]

def gated_delta_scan(q, k, v, g, beta, S0):
    def step(S, inp):
        q_t, k_t, v_t, g_t, b_t = inp
        S = S * jnp.exp(g_t)[..., None, None]
        kv_mem = jnp.einsum('bhkv,bhk->bhv', S, k_t)
        delta = (v_t - kv_mem) * b_t[..., None]
        S = S + jnp.einsum('bhk,bhv->bhkv', k_t, delta)
        o_t = jnp.einsum('bhkv,bhk->bhv', S, q_t)
        return S, o_t
    xs = (jnp.moveaxis(q, 1, 0), jnp.moveaxis(k, 1, 0), jnp.moveaxis(v, 1, 0),
          jnp.moveaxis(g, 1, 0), jnp.moveaxis(beta, 1, 0))
    S, o = lax.scan(step, S0, xs)
    return jnp.moveaxis(o, 0, 1), S

def gated_delta_chunked(q, k, v, g, beta, S0):
    bsz, t, h, dk = q.shape
    dv = v.shape[-1]
    c = GDN_CHUNK
    n = t // c

    def to_chunks(a):
        a = a.reshape((bsz, n, c, h) + a.shape[3:])
        return jnp.moveaxis(a, (1, 3), (0, 2))

    qc, kc, vc, gc, bc = to_chunks(q), to_chunks(k), to_chunks(v), to_chunks(g), to_chunks(beta)
    gcum = jnp.cumsum(gc, axis=-1)
    tril = jnp.tril(jnp.ones((c, c), dtype=bool))
    strict = jnp.tril(jnp.ones((c, c), dtype=bool), -1)
    diff = gcum[..., :, None] - gcum[..., None, :]
    decay_mask = jnp.exp(jnp.where(tril, diff, -jnp.inf))
    kb = kc * bc[..., None]
    vb = vc * bc[..., None]
    a_mat = jnp.where(strict, jnp.einsum('nbhik,nbhjk->nbhij', kb, kc) * decay_mask, 0.0)
    eye = jnp.eye(c, dtype=q.dtype)
    rhs = jnp.concatenate([vb, kb * jnp.exp(gcum)[..., None]], axis=-1)
    sol = lax.linalg.triangular_solve(a_mat + eye, rhs, left_side=True, lower=True)
    u, w = sol[..., :dv], sol[..., dv:]
    qk = jnp.where(tril, jnp.einsum('nbhik,nbhjk->nbhij', qc, kc) * decay_mask, 0.0)

    def step(S, inp):
        q_i, k_i, u_i, w_i, qk_i, g_i = inp
        v_new = u_i - jnp.einsum('bhck,bhkv->bhcv', w_i, S)
        o = (jnp.einsum('bhck,bhkv->bhcv', q_i * jnp.exp(g_i)[..., None], S)
             + jnp.einsum('bhij,bhjv->bhiv', qk_i, v_new))
        g_last = g_i[..., -1]
        k_dec = k_i * jnp.exp(g_last[..., None] - g_i)[..., None]
        S = S * jnp.exp(g_last)[..., None, None] + jnp.einsum('bhck,bhcv->bhkv', k_dec, v_new)
        return S, o

    S, o = lax.scan(step, S0, (qc, kc, u, w, qk, gcum))
    o = jnp.moveaxis(o, (0, 2), (1, 3)).reshape(bsz, t, h, dv)
    return o, S

def gdn_mixer(x, S0, conv_buf, w_in, conv_w, a_log, dt_bias, norm_w, w_out, chunked):
    f32 = jnp.float32
    bsz, t, _ = x.shape
    proj = x @ w_in
    qkv = proj[..., :GDN_CONV_CH]
    z = proj[..., GDN_CONV_CH:GDN_CONV_CH + GDN_V_W]
    a = proj[..., GDN_CONV_CH + GDN_V_W:GDN_CONV_CH + GDN_V_W + GDN_HEADS]
    b = proj[..., GDN_CONV_CH + GDN_V_W + GDN_HEADS:]
    qkv_c, new_buf = causal_dwconv(qkv, conv_buf, conv_w)
    qkv_c = jax.nn.silu(qkv_c.astype(f32))
    q = qkv_c[..., :GDN_QK_W].reshape(bsz, t, GDN_HEADS, GDN_DK)
    k = qkv_c[..., GDN_QK_W:2 * GDN_QK_W].reshape(bsz, t, GDN_HEADS, GDN_DK)
    v = qkv_c[..., 2 * GDN_QK_W:].reshape(bsz, t, GDN_HEADS, GDN_DV)
    q = l2_normalize(q) * (GDN_DK ** -0.5)
    k = l2_normalize(k)
    g = -jnp.exp(a_log.astype(f32)) * jax.nn.softplus(a.astype(f32) + dt_bias.astype(f32))
    beta = jax.nn.sigmoid(b.astype(f32))
    S0f = S0.astype(f32)
    if chunked:
        o, S = gated_delta_chunked(q, k, v, g, beta, S0f)
    else:
        o, S = gated_delta_scan(q, k, v, g, beta, S0f)
    o = o * lax.rsqrt(jnp.mean(jnp.square(o), axis=-1, keepdims=True) + NORM_EPS) * norm_w.astype(f32)
    o = o * jax.nn.silu(z.astype(f32)).reshape(bsz, t, GDN_HEADS, GDN_DV)
    y = o.reshape(bsz, t, GDN_V_W).astype(x.dtype) @ w_out
    return y, S.astype(S0.dtype), new_buf

def shortconv_mixer(x, buf, w_in, conv_w, w_out):
    proj = x @ w_in
    b_gate, c_gate, h = jnp.split(proj, 3, axis=-1)
    conv, new_buf = causal_dwconv(c_gate * h, buf, conv_w)
    return (b_gate * conv) @ w_out, new_buf

def swiglu(x, w_gu, w_down):
    gate, up = jnp.split(x @ w_gu, 2, axis=-1)
    return (jax.nn.silu(gate) * up) @ w_down

def moe_swiglu(x, w_router, w_gu, w_down):
    logits = (x @ w_router).astype(jnp.float32)
    top_v, top_i = lax.top_k(logits, TOP_K)
    gates = jax.nn.softmax(top_v, axis=-1)
    combine = jnp.einsum('...k,...ke->...e', gates, jax.nn.one_hot(top_i, N_EXPERTS, dtype=jnp.float32))
    y = jnp.zeros_like(x)
    for e in range(N_EXPERTS):
        y = y + swiglu(x, w_gu[e], w_down[e]) * combine[..., e:e + 1].astype(x.dtype)
    return y

def setup_inputs(seed: int = 0) -> dict:
    key = jax.random.key(seed)
    ks = jax.random.split(key, 24)
    nrm = lambda k, shape, s: jax.random.normal(k, shape, jnp.float32) * s
    dt = jnp.exp(jax.random.uniform(ks[9], (N_EVEN_LAYERS, GDN_HEADS), jnp.float32,
                                    minval=math.log(1e-3), maxval=math.log(1e-1)))
    return {
        'x_prompt': nrm(ks[0], (BATCH, SEQ, D_MODEL), 1.0),
        'x_sample': nrm(ks[1], (DEC_BATCH, DEC_SEQ, D_MODEL), 1.0),
        'state_gdn_S': nrm(ks[2], (N_EVEN_LAYERS, DEC_BATCH, GDN_HEADS, GDN_DK, GDN_DV), 0.1),
        'state_gdn_conv': nrm(ks[3], (N_EVEN_LAYERS, DEC_BATCH, GDN_CONV - 1, GDN_CONV_CH), 1.0),
        'state_sconv': nrm(ks[4], (N_ODD_LAYERS, DEC_BATCH, SC_WIDTH - 1, D_MODEL), 1.0),
        'ln_g': 1.0 + nrm(ks[5], (DEPTH, 2, D_MODEL), 0.02),
        'ln_b': nrm(ks[6], (DEPTH, 2, D_MODEL), 0.02),
        'gdn_w_in': nrm(ks[7], (N_EVEN_LAYERS, D_MODEL, GDN_IN_COLS), D_MODEL ** -0.5),
        'gdn_conv_w': nrm(ks[8], (N_EVEN_LAYERS, GDN_CONV, GDN_CONV_CH), GDN_CONV ** -0.5),
        'gdn_a_log': jnp.log(jax.random.uniform(ks[10], (N_EVEN_LAYERS, GDN_HEADS), jnp.float32,
                                                minval=1.0, maxval=16.0)),
        'gdn_dt_bias': dt + jnp.log(-jnp.expm1(-dt)),
        'gdn_norm_w': 1.0 + nrm(ks[11], (N_EVEN_LAYERS, GDN_DV), 0.02),
        'gdn_w_out': nrm(ks[12], (N_EVEN_LAYERS, GDN_V_W, D_MODEL), GDN_V_W ** -0.5 * BETA_INIT),
        'sc_w_in': nrm(ks[13], (N_ODD_LAYERS, D_MODEL, 3 * D_MODEL), D_MODEL ** -0.5),
        'sc_conv_w': nrm(ks[14], (N_ODD_LAYERS, SC_WIDTH, D_MODEL), SC_WIDTH ** -0.5),
        'sc_w_out': nrm(ks[15], (N_ODD_LAYERS, D_MODEL, D_MODEL), D_MODEL ** -0.5 * BETA_INIT),
        'ffn_w_gu': nrm(ks[16], (N_EVEN_LAYERS, D_MODEL, 2 * D_FF), D_MODEL ** -0.5),
        'ffn_w_down': nrm(ks[17], (N_EVEN_LAYERS, D_FF, D_MODEL), D_FF ** -0.5 * BETA_INIT),
        'moe_w_router': nrm(ks[18], (N_ODD_LAYERS, D_MODEL, N_EXPERTS), D_MODEL ** -0.5),
        'moe_w_gu': nrm(ks[19], (N_ODD_LAYERS, N_EXPERTS, D_MODEL, 2 * D_FF_EXPERT), D_MODEL ** -0.5),
        'moe_w_down': nrm(ks[20], (N_ODD_LAYERS, N_EXPERTS, D_FF_EXPERT, D_MODEL),
                          D_FF_EXPERT ** -0.5 * BETA_INIT),
    }

def reference(x_prompt, x_sample, state_gdn_S, state_gdn_conv, state_sconv, ln_g, ln_b,
              gdn_w_in, gdn_conv_w, gdn_a_log, gdn_dt_bias, gdn_norm_w, gdn_w_out,
              sc_w_in, sc_conv_w, sc_w_out, ffn_w_gu, ffn_w_down, moe_w_router, moe_w_gu, moe_w_down):
    hp, hs = x_prompt, x_sample
    bp = x_prompt.shape[0]
    s_p, s_s, cv_p, cv_s, sc_p, sc_s = [], [], [], [], [], []
    for i in range(DEPTH):
        j = i // 2
        if i % 2 == 0:
            w = (gdn_w_in[j], gdn_conv_w[j], gdn_a_log[j], gdn_dt_bias[j], gdn_norm_w[j], gdn_w_out[j])
            S0p = jnp.zeros((bp,) + state_gdn_S.shape[2:], state_gdn_S.dtype)
            buf0p = jnp.zeros((bp,) + state_gdn_conv.shape[2:], state_gdn_conv.dtype)
            mp, sp_new, cp_new = gdn_mixer(hp, S0p, buf0p, *w, chunked=True)
            ms, ss_new, cs_new = gdn_mixer(hs, state_gdn_S[j], state_gdn_conv[j], *w, chunked=False)
            s_p.append(sp_new); s_s.append(ss_new); cv_p.append(cp_new); cv_s.append(cs_new)
        else:
            buf0p = jnp.zeros((bp,) + state_sconv.shape[2:], state_sconv.dtype)
            mp, bp_new = shortconv_mixer(hp, buf0p, sc_w_in[j], sc_conv_w[j], sc_w_out[j])
            ms, bs_new = shortconv_mixer(hs, state_sconv[j], sc_w_in[j], sc_conv_w[j], sc_w_out[j])
            sc_p.append(bp_new); sc_s.append(bs_new)
        hp = layer_norm(ALPHA * hp + mp, ln_g[i, 0], ln_b[i, 0])
        hs = layer_norm(ALPHA * hs + ms, ln_g[i, 0], ln_b[i, 0])
        if i % 2 == 0:
            fp = swiglu(hp, ffn_w_gu[j], ffn_w_down[j])
            fs = swiglu(hs, ffn_w_gu[j], ffn_w_down[j])
        else:
            fp = moe_swiglu(hp, moe_w_router[j], moe_w_gu[j], moe_w_down[j])
            fs = moe_swiglu(hs, moe_w_router[j], moe_w_gu[j], moe_w_down[j])
        hp = layer_norm(ALPHA * hp + fp, ln_g[i, 1], ln_b[i, 1])
        hs = layer_norm(ALPHA * hs + fs, ln_g[i, 1], ln_b[i, 1])
    gdn_S_prompt = jnp.stack(s_p)
    gdn_S_sample = jnp.stack(s_s)
    gdn_conv_prompt = jnp.stack(cv_p)
    gdn_conv_sample = jnp.stack(cv_s)
    sconv_prompt = jnp.stack(sc_p)
    sconv_sample = jnp.stack(sc_s)
    return (hp, hs, gdn_S_prompt, gdn_S_sample, gdn_conv_prompt, gdn_conv_sample, sconv_prompt, sconv_sample)


_drawn_inputs = setup_inputs


def setup_inputs(seed=0):
    import zlib

    import numpy as np

    out = dict(_drawn_inputs(seed))
    spreads = {}
    factors = {'gdn_norm_w': 7.139}
    for name, (base, spread) in spreads.items():
        noise = np.random.default_rng([zlib.crc32(name.encode()), seed]).standard_normal(out[name].shape)
        drawn = base * np.exp(spread * noise) if base else spread * noise
        out[name] = __import__('jax').numpy.asarray(drawn.astype(out[name].dtype))
    for name, factor in factors.items():
        out[name] = (out[name] * factor).astype(out[name].dtype)
    return out
```

```python
import concourse.bass as bass
from concourse import mybir
from contextlib import ExitStack
import math

D = 1024
KT = D // 128
NP, NS = 256, 8
N = NP + NS
HEADS = 8
CH = 128
NCH = NP // CH
LEVELS = 7
TAPS = 4
QKV = 3 * D
QT = QKV // 128
SCW = 3
FF = 2816
FT = FF // 128
EX = 8
FE = 3584
ALPHA = 4.0 ** 0.25
LN_EPS, NORM_EPS = 1e-5, 1e-6
SLOT = 2048
RAW, SPLIT = 6, 3
UNITS = FE // 512
EXPERT_SLOTS = 6 * UNITS
CAP = 128
TILES = -(-N // CAP)

IN0 = 0
OUT0 = IN0 + 4 * D // 256
GU0 = OUT0 + D // 256
DOWN0 = GU0 + 2 * FF // 256
SCI0 = DOWN0 + FF // 256
SCO0 = SCI0 + 3 * D // 256
MOE0 = SCO0 + D // 256


WORDS = 53184


class Steps:

    def __init__(self, engine, semaphore, base=0):
        self.engine, self.semaphore, self.base, self.count = engine, semaphore, base, 0

    def __call__(self, instruction):
        instruction.then_inc(self.semaphore, 1)
        self.count += 1
        return instruction

    def wait(self):
        self.engine.wait_ge(self.semaphore, self.base + self.count)


def hybrid_step(nc, x_prompt, x_sample, state_gdn_S, state_gdn_conv, state_sconv, ln_g, ln_b, gdn_w_in,
                gdn_conv_w, gdn_a_log, gdn_dt_bias, gdn_norm_w, gdn_w_out, sc_w_in, sc_conv_w, sc_w_out,
                ffn_w_gu, ffn_w_down, moe_w_router, moe_w_gu, moe_w_down,
                y_prompt, y_sample, S_prompt, S_sample, conv_prompt, conv_sample, sconv_prompt, sconv_sample):
    F32, F32R, I32 = mybir.dt.float32, mybir.dt.float32r, mybir.dt.int32
    ALU = mybir.AluOpType
    ACT = mybir.ActivationFunctionType
    X = mybir.AxisListType.X

    with ExitStack() as ctx:
        base = -(-nc.sbuf_base // 32) * 32
        ctx.enter_context(nc.sbuf_tensor("arena", [128, WORDS], F32))
        cursor = [base]

        def place(name, shape, dtype=F32, at=None):
            size = 4 * math.prod(shape[1:])
            size += -size % 32
            offset = cursor[0] if at is None else at
            if at is None:
                cursor[0] += size
            assert offset + size <= base + WORDS * 4, (name, offset + size - base)
            return nc.alloc_sbuf_tensor_at(name, shape, dtype, offset=offset)

        def sem(name):
            return ctx.enter_context(nc.semaphore(name))

        raw = place("raw", [128, RAW, SLOT])
        high = place("high", [128, SPLIT, SLOT], F32R)
        low = place("low", [128, SPLIT, SLOT], F32R)
        ident = place("ident", [128, 128])
        ones = place("ones", [128, 128])
        upper = place("upper", [128, 128])
        level_mask = place("level_mask", [128, LEVELS, 128])
        taps = place("taps", [128, QT, 28])
        vecs = place("vecs", [128, KT, 27])
        norm_w = place("norm_w", [128, 1])
        eps = place("eps", [128, 2])
        wab = place("wab", [128, KT, 16])
        wr = place("wr", [128, KT, EX])
        a_log = place("a_log", [8, 1])
        dt_bias = place("dt_bias", [8, 1])
        xres = place("xres", [128, KT, N])
        xs_at = cursor[0]
        xh = place("xh", [128, KT, N], F32R)
        xl = place("xl", [128, KT, N], F32R)
        region = cursor[0]

        qkv = place("qkv", [128, QT, N])
        zgate = place("zgate", [128, KT, N])
        g3_at = cursor[0]
        gB = place("gB", [128, HEADS, CH])
        bB = place("bB", [128, HEADS, CH])
        egB = place("egB", [128, HEADS, CH])
        S = place("S", [128, HEADS, 128])
        t_at = cursor[0]
        T = place("T", [128, HEADS, CH])
        TT = place("TT", [128, HEADS, CH])
        P1 = place("P1", [128, HEADS, CH])
        ATm = place("ATm", [128, HEADS, CH])
        u_at = cursor[0]
        U = place("U", [128, 4, TAPS - 1 + N])
        utail = place("utail", [128, QT, 11])
        s_at = cursor[0]
        gg = place("gg", [8, N])
        beta = place("beta", [8, N])
        gcol = place("gcol", [128, 2, 2, HEADS])
        nbe = place("nbe", [128, NCH, HEADS])
        kd = place("kd", [128, NCH, HEADS])
        aS = place("aS", [128, HEADS, NS])
        bS = place("bS", [128, HEADS, NS])
        kq = place("kq", [128, HEADS, NS])
        delta = place("delta", [128, HEADS, NS])
        tmpS = place("tmpS", [128, HEADS, NS])
        sconv_tmp = place("sconv_tmp", [128, QT, NS])
        layer0_end = cursor[0]
        xnat = place("xnat", [128, 2, D], at=g3_at)
        xsnat = place("xsnat", [8, D], at=g3_at + 8 * D)
        taps_nat = place("taps_nat", [28, QKV], at=g3_at + 12 * D)
        vecs_nat = place("vecs_nat", [27, D], at=g3_at + 24 * D)
        sp = [place(f"sp{i}", [8, N], at=region + 4 * QT * N + i * 8 * N) for i in range(2)]
        tail_nat = place("tail_nat", [11, QKV], at=xs_at)
        s0a = place("s0a", [128, 4, HEADS, 128], at=g3_at)
        s0b = place("s0b", [128, 4, HEADS, 128], at=t_at)
        kn_s = place("kn_s", [8, D], at=u_at)
        Kn = place("Kn", [128, HEADS, 128], at=xs_at)
        Vn = place("Vn", [128, HEADS, 128], at=xs_at + 4 * D)
        AT = place("AT", [128, HEADS, CH], at=xs_at + 8 * D)
        DM = place("DM", [128, HEADS, CH], at=xs_at + 12 * D)
        osq = place("osq", [128, KT, N], at=t_at)
        ln_at = base + WORDS * 4 - 4 * (KT * N + 3 * N) - 64
        ln_at -= (ln_at - base) % 32
        lnsq = place("lnsq", [128, KT, N], at=ln_at)
        squares = place("squares", [128, 2, 4, N], at=t_at)
        dmask = place("dmask", [8, 2, 4, 128], at=xs_at + 12 * D)
        mu = place("mu", [128, N], at=ln_at + 4 * KT * N)
        rstd = place("rstd", [128, N], at=ln_at + 4 * (KT + 1) * N)
        rvar = place("rvar", [128, N], at=ln_at + 4 * (KT + 2) * N)
        hh = place("hh", [128, FT, N], F32R, at=region)
        hl = place("hl", [128, FT, N], F32R, at=region + 4 * FT * N)
        sg = place("sg", [128, 4, N], at=region + 8 * FT * N)
        hf = place("hf", [128, 4, N], at=region + 8 * FT * N + 16 * N)
        su = place("su", [128, KT, SCW - 1 + N], at=region)
        sc = place("sc", [128, KT, N], at=region + 9 * D)
        cc = place("cc", [128, 4, N], at=region + 18 * D)
        sy = place("sy", [128, 4, N], at=region + 23 * D)
        yh = place("yh", [128, KT, N], F32R, at=region + 28 * D)
        yl = place("yl", [128, KT, N], F32R, at=region + 37 * D)
        stail_nat = place("stail_nat", [10, D], at=region + 46 * D)
        xnh = place("xnh", [128, 3, D], F32R, at=region)
        xnl = place("xnl", [128, 3, D], F32R, at=region + 12 * D)
        hx = place("hx", [128, 2, 512], at=region + 24 * D)
        sgx = place("sgx", [128, 2, 512], at=region + 28 * D)
        hth = place("hth", [128, 2, 512], F32R, at=region + 32 * D)
        htl = place("htl", [128, 2, 512], F32R, at=region + 36 * D)
        yxh = place("yxh", [128, D], F32R, at=region + 40 * D)
        yxl = place("yxl", [128, D], F32R, at=region + 44 * D)
        m_at = region + 48 * D
        pick = place("pick", [128, 3, CAP], F32R, at=m_at)
        pickg = place("pickg", [128, 3, CAP], at=m_at + 1536)
        pth = place("pth", [128, N], F32R, at=m_at + 3072)
        ptl = place("ptl", [128, N], F32R, at=m_at + 3072 + 1056)
        iota_i = place("iota_i", [128, CAP], I32, at=m_at + 5184)
        iota_f = place("iota_f", [128, CAP], at=m_at + 5184 + 512)
        tab_at = m_at + 6208
        JOBS = EX * TILES + 1
        slot_tab = place("slot_tab", [128, JOBS, 3], at=tab_at)
        gate_tab = place("gate_tab", [128, JOBS, 3], at=tab_at + 320)
        logits = place("logits", [128, 3, EX], at=tab_at + 640)
        sel = place("sel", [128, 3, EX], at=tab_at + 736)
        gates = place("gates", [128, 3, EX], at=tab_at + 832)
        rank = place("rank", [128, 3, EX], at=tab_at + 928)
        valid = place("valid", [128, 3, EX], at=tab_at + 1024)
        cmp_gt = place("cmp_gt", [128, 3, EX, EX], at=tab_at + 1120)
        cmp_eq = place("cmp_eq", [128, 3, EX, EX], at=tab_at + 1888)
        before = place("before", [128, EX, EX], at=tab_at + 2656)
        top = place("top", [128, 3], at=tab_at + 2912)
        total = place("total", [128, EX], at=tab_at + 2944)
        most = place("most", [128, 4], at=tab_at + 2976)
        tiles_i = place("tiles_i", [1, 1], I32, at=tab_at + 3008)
        scol = place("scol", [128, 3], at=tab_at + 3040)
        scol_g = place("scol_g", [128, 3], at=tab_at + 3072)
        gcol_g = place("gcol_g", [128, 3], at=tab_at + 3104)
        xgh = place("xgh", [128, KT, CAP], F32R, at=xs_at)
        xgl = place("xgl", [128, KT, CAP], F32R, at=xs_at + 4 * D)
        ynat = place("ynat", [128, 3, D], at=region)

        bank = [ctx.enter_context(nc.psum_tensor(f"bank{i}", [128, 512], F32)) for i in range(8)]

        def heads(b):
            return bank[b][:, :].rearrange("p (h i) -> p h i", h=4)

        raw_in = [sem(f"raw_in{i}") for i in range(RAW)]
        high_ready, low_ready, slot_used = sem("high_ready"), sem("low_ready"), sem("slot_used")
        x_in, nat_in, small_in, s0a_in, s0b_in = sem("x_in"), sem("nat_in"), sem("small_in"), sem("s0a_in"), sem("s0b_in")
        hist_out = sem("hist_out")
        const_ready, mask_ready, pool_step = sem("const_ready"), sem("mask_ready"), sem("pool_step")
        dve_step, act_step = sem("dve_step"), sem("act_step")
        xT_psum, xh_ready, xl_ready = sem("xT_psum"), sem("xh_ready"), sem("xl_ready")
        nat_T, taps_ready, ab_psum = sem("nat_T"), sem("taps_ready"), sem("ab_psum")
        proj_out, conv_done, silu_done, tail_psum, tail_sb, tail_out = (
            sem("proj_out"), sem("conv_done"), sem("silu_done"), sem("tail_psum"), sem("tail_sb"), sem("tail_out"))
        sq_ready, sq_psum, sq_log, sq_inv, z_ready, qk_ready = (
            sem("sq_ready"), sem("sq_psum"), sem("sq_log"), sem("sq_inv"), sem("z_ready"), sem("qk_ready"))
        gate_a, gate_b, gate_c, gate_ready, gcol_psum, gcol_ready, nbe_ready, aS_ready = (
            sem("gate_a"), sem("gate_b"), sem("gate_c"), sem("gate_ready"), sem("gcol_psum"), sem("gcol_ready"),
            sem("nbe_ready"), sem("aS_ready"))
        dec_psum, kq_ready, delta_ready, dn_psum, kn_ready, dmask_ready, outer_psum, s_updated, sa_out, sb_out = (
            sem("dec_psum"), sem("kq_ready"), sem("delta_ready"), sem("dn_psum"), sem("kn_ready"), sem("dmask_ready"),
            sem("outer_psum"), sem("s_updated"), sem("sa_out"), sem("sb_out"))
        bc_psum, g_act, b_dve, kk_psum, d_ready, e_ready, at_ready, atm_ready, p1_psum, p1_ready, dd_psum, t_ready = (
            sem("bc_psum"), sem("g_act"), sem("b_dve"), sem("kk_psum"), sem("d_ready"), sem("e_ready"), sem("at_ready"),
            sem("atm_ready"), sem("p1_psum"), sem("p1_ready"), sem("dd_psum"), sem("t_ready"))
        nat_psum, kv_nat, tt1_ready, t1_psum, ks_psum, r_ready, vn_psum, vn_ready, oS_psum, o_ready, s_ready = (
            sem("nat_psum"), sem("kv_nat"), sem("tt1_ready"), sem("t1_psum"), sem("ks_psum"), sem("r_ready"),
            sem("vn_psum"), sem("vn_ready"), sem("oS_psum"), sem("o_ready"), sem("s_ready"))
        osq_ready, osq_psum, o_inv, o_root, on_ready = (
            sem("osq_ready"), sem("osq_psum"), sem("o_inv"), sem("o_root"), sem("on_ready"))
        res_ready, mean_psum, xc_ready, lnsq_ready, var_psum, var_inv, var_root, scaled, x_new = (
            sem("res_ready"), sem("mean_psum"), sem("xc_ready"), sem("lnsq_ready"), sem("var_psum"), sem("var_inv"),
            sem("var_root"), sem("scaled"), sem("x_new"))
        gate_silu, h_ready, hh_ready, hl_ready = sem("gate_silu"), sem("h_ready"), sem("hh_ready"), sem("hl_ready")
        c_copied, u_ready, sconv_ready, sy_ready, yh_ready, yl_ready = (
            sem("c_copied"), sem("u_ready"), sem("sconv_ready"), sem("sy_ready"), sem("yh_ready"), sem("yl_ready"))
        stail_psum, stail_sb, stail_out = sem("stail_psum"), sem("stail_sb"), sem("stail_out")
        logit_psum, top_ready, ex_ready, sel_ready, rank_psum, tiles_ready, xn_psum, xnh_ready, xnl_ready = (
            sem("logit_psum"), sem("top_ready"), sem("ex_ready"), sem("sel_ready"), sem("rank_psum"),
            sem("tiles_ready"), sem("xn_psum"), sem("xnh_ready"), sem("xnl_ready"))
        pick_ready, pickg_ready, xg_psum, xgh_ready, xgl_ready, pt_psum, pth_ready, ptl_ready = (
            sem("pick_ready"), sem("pickg_ready"), sem("xg_psum"), sem("xgh_ready"), sem("xgl_ready"), sem("pt_psum"),
            sem("pth_ready"), sem("ptl_ready"))
        sgx_ready, hx_ready, ht_psum, hth_ready, htl_ready, yxh_ready, yxl_ready, scat_psum, scat_done, moe_step = (
            sem("sgx_ready"), sem("hx_ready"), sem("ht_psum"), sem("hth_ready"), sem("htl_ready"), sem("yxh_ready"),
            sem("yxl_ready"), sem("scat_psum"), sem("scat_done"), sem("moe_step"))
        y_psum, y_sb, y_out = sem("y_psum"), sem("y_sb"), sem("y_out")

        def cols(w, at, n=256):
            return w[:, at:at + n].rearrange("(k p) f -> p k f", p=128)

        dense = [cols(gdn_w_in[0], 256 * i) for i in range(4 * D // 256)]
        dense += [cols(gdn_w_out[0], 256 * i) for i in range(D // 256)]
        for i in range(FF // 256):
            dense += [cols(ffn_w_gu[0], 256 * i), cols(ffn_w_gu[0], FF + 256 * i)]
        dense += [ffn_w_down[0, 256 * i:256 * i + 256, :].rearrange("(k p) f -> p k f", p=128) for i in range(FF // 256)]
        for i in range(D // 256):
            dense += [cols(sc_w_in[0], D + 256 * i), cols(sc_w_in[0], 2 * D + 256 * i)]
        dense += [cols(sc_w_in[0], 256 * i) for i in range(D // 256)]
        dense += [cols(sc_w_out[0], 256 * i) for i in range(D // 256)]
        assert len(dense) == MOE0 and MOE0 % SPLIT == 0 and EXPERT_SLOTS % RAW == 0 and EXPERT_SLOTS % SPLIT == 0

        def unit_first(u):
            return 0 if u == 0 else 4 + 6 * (u - 1)

        def down_first(u):
            return 8 + 6 * u if u < UNITS - 1 else EXPERT_SLOTS - 2

        def load(eng, n, src, before=0):
            r = n % RAW
            dst = raw[:, r, :].rearrange("p (k f) -> p k f", k=src.shape[1])
            if not isinstance(before, int) or n >= RAW:
                eng.wait_ge(low_ready, before + (n - RAW + 1))
            eng.dma_start(dst, src).then_inc(raw_in[r], 16)

        def split_high(eng, n, before=0, rounds=0):
            eng.wait_ge(raw_in[n % RAW], rounds + 16 * (n // RAW + 1))
            if n >= SPLIT:
                eng.wait_ge(slot_used, before + (n - SPLIT + 1))
            eng.activation(high[:, n % SPLIT, :], raw[:, n % RAW, :], ACT.Copy).then_inc(high_ready, 1)

        def split_low(eng, n, before=0):
            eng.wait_ge(high_ready, before + (n + 1))
            eng.tensor_tensor(low[:, n % SPLIT, :], raw[:, n % RAW, :], high[:, n % SPLIT, :].bitcast(F32),
                              ALU.subtract).then_inc(low_ready, 1)

        def dense_slot(pe, n, b, act_h, act_l):
            wh = high[:, n % SPLIT, :].rearrange("p (k f) -> p k f", k=KT)
            wl = low[:, n % SPLIT, :].rearrange("p (k f) -> p k f", k=KT)
            pe.wait_ge(high_ready, n + 1)
            for t in range(2):
                f = slice(128 * t, 128 * t + 128)
                out = bank[b + t][:, 0:N]
                for k in range(KT):
                    pe.matmul(out, wh[:, k, f], act_h[:, k, :], start=k == 0, stop=False)
                    pe.matmul(out, wh[:, k, f], act_l[:, k, :], start=False, stop=False)
                if t == 0:
                    pe.wait_ge(low_ready, n + 1)
                for k in range(KT):
                    last = pe.matmul(out, wl[:, k, f], act_h[:, k, :], start=False, stop=k == KT - 1)
            last.then_inc(slot_used, 1)

        lns = [(0, 1), (1, 2), (2, None), (3, None)]

        def ln_row(l):
            return l, 4 + l

        block = ctx.enter_context(nc.Block())

        @block.sync
        def _(sp_):
            sp_.dma_start(xnat[:, :, :], x_prompt[0].rearrange("(c p) d -> p c d", p=128)).then_inc(x_in, 16)
            sp_.dma_start(xsnat[:, :], x_sample[:, 0, :]).then_inc(x_in, 16)
            for n, src in enumerate(dense):
                load(sp_, n, src)
            tiles = sp_.alloc_register("sp_tiles")
            sp_.reg_mov(tiles, 1)
            with sp_.Fori(0, tiles) as t:
                with sp_.Fori(0, EX) as e:
                    job = t * EX + e
                    done = job * EXPERT_SLOTS

                    def gate_up(u):
                        for w in range(2):
                            for kh in range(2):
                                n = MOE0 + unit_first(u) + 2 * w + kh
                                at = w * FE + 512 * u
                                load(sp_, n, moe_w_gu[0, bass.ds(e, 1), 512 * kh:512 * kh + 512, at:at + 512]
                                     .rearrange("a (k p) f -> p (a k) f", p=128), before=done)

                    def down(u):
                        for kh in range(2):
                            n = MOE0 + down_first(u) + kh
                            at = 512 * u + 256 * kh
                            load(sp_, n, moe_w_down[0, bass.ds(e, 1), at:at + 256, :]
                                 .rearrange("a (k p) f -> p (a k) f", p=128), before=done)

                    for u in range(UNITS):
                        gate_up(u)
                        if u:
                            down(u - 1)
                    down(UNITS - 1)
                sp_.wait_ge(tiles_ready, 1)
                sp_.reg_load(tiles, tiles_i[0:1, 0:1])

        @block.gpsimd
        def _(pool):
            step = Steps(pool, pool_step)
            pool.memset(ident[:, :], 0.0).then_inc(pool_step, 1)
            pool.memset(ones[:, :], 1.0).then_inc(const_ready, 1)
            pool.memset(eps[:, 0:1], NORM_EPS).then_inc(const_ready, 1)
            pool.memset(eps[:, 1:2], LN_EPS).then_inc(const_ready, 1)
            step.count = 1
            step.wait()
            pool.affine_select(out=ident[:, :], in_=ident[:, :], compare_op=ALU.not_equal, fill=1.0, base=0,
                               pattern=[[-1, 128]], channel_multiplier=1).then_inc(const_ready, 1)
            pool.memset(U[:, :, 0:TAPS - 1], 0.0).then_inc(const_ready, 1)
            step(pool.memset(upper[:, :], 1.0))
            step(pool.memset(level_mask[:, :, :], 0.0))
            step.wait()
            pool.affine_select(out=upper[:, :], in_=upper[:, :], compare_op=ALU.is_ge, fill=0.0, base=0,
                               pattern=[[1, 128]], channel_multiplier=-1).then_inc(mask_ready, 1)
            for s in range(LEVELS):
                b, blocks = 1 << s, CH >> (s + 1)
                v = level_mask[:, s, :].rearrange("p (n h r) -> p n h r", h=2, r=b)[:, :, 1, :]
                step(pool.memset(v, 1.0))
                step.wait()
                step(pool.affine_select(out=v, in_=v, compare_op=ALU.is_ge, fill=0.0, base=0,
                                        pattern=[[-2 * b, blocks], [0, b]], channel_multiplier=1))
                step.wait()
                pool.affine_select(out=v, in_=v, compare_op=ALU.is_ge, fill=0.0, base=b - 1,
                                   pattern=[[2 * b, blocks], [0, b]], channel_multiplier=-1).then_inc(mask_ready, 1)
            pool.dma_start(conv_sample[0, :, 0:TAPS - 2, :], state_gdn_conv[0, :, 1:TAPS - 1, :]).then_inc(hist_out, 16)
            pool.dma_start(sconv_sample[0, :, 0:SCW - 2, :], state_sconv[0, :, 1:SCW - 1, :]).then_inc(hist_out, 16)
            pool.wait_ge(tail_sb, 6)
            pool.dma_start(conv_prompt[0, 0, :, :], tail_nat[0:3, :]).then_inc(tail_out, 16)
            pool.dma_start(conv_sample[0, :, TAPS - 2, :], tail_nat[3:11, :]).then_inc(tail_out, 16)
            for half, (s0, s_out) in enumerate(((s0a, sa_out), (s0b, sb_out))):
                pool.wait_ge(s_updated, HEADS * (half + 1))
                for i in range(4):
                    pool.dma_start(S_sample[0, 4 * half + i].rearrange("h k v -> k h v"), s0[:, i, :, :])\
                        .then_inc(s_out, 16)
            pool.wait_ge(mask_ready, 1 + LEVELS)
            for c in range(NCH):
                for s in range(LEVELS):
                    for g in range(2):
                        if s == 0:
                            pool.wait_ge(at_ready, 2 * c + g + 1)
                            if c:
                                pool.wait_ge(p1_psum, 2 * (LEVELS - 1) * c)
                            else:
                                pool.wait_ge(sb_out, 64)
                        elif s == 1:
                            pool.wait_ge(tt1_ready, 2 * c + g + 1)
                        else:
                            pool.wait_ge(p1_psum, 2 * (LEVELS - 1) * c + 2 * (s - 2) + g + 1)
                        hs = slice(4 * g, 4 * g + 4)
                        pool.tensor_tensor(ATm[:, hs, :], AT[:, hs, :],
                                           level_mask[:, s:s + 1, :].to_broadcast([128, 4, CH]),
                                           ALU.mult).then_inc(atm_ready, 1)
            pool.wait_ge(s_ready, 2 * NCH)
            pool.dma_start(S_prompt[0, 0].rearrange("h k v -> k h v"), S[:, :, :]).then_inc(hist_out, 16)
            pool.wait_ge(xl_ready, 8 * 4)
            pool.memset(su[:, :, 0:SCW - 1], 0.0).then_inc(const_ready, 1)
            pool.wait_ge(stail_sb, 2)
            pool.dma_start(sconv_prompt[0, 0, :, :], stail_nat[0:2, :]).then_inc(stail_out, 16)
            pool.dma_start(sconv_sample[0, :, SCW - 2, :], stail_nat[2:10, :]).then_inc(stail_out, 16)
            pool.wait_ge(slot_used, MOE0)
            pool.wait_ge(stail_out, 32)
            step(pool.iota(iota_i[:, :], pattern=[[1, CAP]], base=0, channel_multiplier=0))
            step(pool.memset(valid[:, :, :], 1.0))
            step(pool.memset(before[:, :, :], 1.0))
            step(pool.memset(slot_tab[:, EX * TILES:JOBS, :], -1.0))
            step(pool.memset(gate_tab[:, EX * TILES:JOBS, :], 0.0))
            step(pool.memset(logits[:, :, :], 0.0))
            step(pool.memset(xnh[:, 2, :].bitcast(F32), 0.0))
            step(pool.memset(xnl[:, 2, :].bitcast(F32), 0.0))
            step.wait()
            step(pool.affine_select(out=valid[:, 2, :], in_=valid[:, 2, :], compare_op=ALU.is_ge, fill=0.0,
                                    base=NS - 1, pattern=[[0, EX]], channel_multiplier=-1))
            step(pool.affine_select(out=before[:, :, :], in_=before[:, :, :], compare_op=ALU.is_ge, fill=0.0,
                                    base=-1, pattern=[[1, EX], [-1, EX]], channel_multiplier=0))
            step.wait()
            pool.tensor_copy(iota_f[:, :], iota_i[:, :]).then_inc(const_ready, 1)
            pool.wait_ge(y_sb, 6)
            pool.dma_start(y_prompt[0].rearrange("(c p) d -> p c d", p=128), ynat[:, 0:2, :]).then_inc(y_out, 16)
            pool.dma_start(y_sample[:, 0, :], ynat[0:8, 2, :]).then_inc(y_out, 16)
            pool.wait_ge(hist_out, 48)
            pool.wait_ge(tail_out, 32)
            pool.wait_ge(sa_out, 64)
            pool.wait_ge(sb_out, 64)
            pool.wait_ge(stail_out, 32)
            pool.wait_ge(y_out, 32)

        @block.scalar
        def _(act):
            for j in range(TAPS - 1):
                act.dma_start(taps_nat[8 * j:8 * j + 8, :], state_gdn_conv[0, :, j, :]).then_inc(nat_in, 16)
            act.dma_start(taps_nat[24:28, :], gdn_conv_w[0]).then_inc(nat_in, 16)
            act.dma_start(vecs_nat[0:4, :], ln_g.rearrange("a b d -> (a b) d")).then_inc(nat_in, 16)
            act.dma_start(vecs_nat[4:8, :], ln_b.rearrange("a b d -> (a b) d")).then_inc(nat_in, 16)
            act.dma_start(vecs_nat[8:11, :], sc_conv_w[0]).then_inc(nat_in, 16)
            for j in range(SCW - 1):
                act.dma_start(vecs_nat[11 + 8 * j:19 + 8 * j, :], state_sconv[0, :, j, :]).then_inc(nat_in, 16)
            act.dma_start(wab[:, :, :], gdn_w_in[0][:, 4 * D:4 * D + 16].rearrange("(k p) f -> p k f", p=128))\
                .then_inc(small_in, 16)
            act.dma_start(wr[:, :, :], moe_w_router[0].rearrange("(k p) f -> p k f", p=128)).then_inc(small_in, 16)
            act.dma_start(norm_w[:, :], gdn_norm_w.rearrange("a v -> v a")).then_inc(small_in, 16)
            act.dma_start(a_log[:, :], gdn_a_log.rearrange("a h -> h a")).then_inc(small_in, 16)
            act.dma_start(dt_bias[:, :], gdn_dt_bias.rearrange("a h -> h a")).then_inc(small_in, 16)
            step = Steps(act, act_step)
            for k in range(KT):
                act.wait_ge(xT_psum, k + 1)
                act.activation(xh[:, k, :], bank[k][:, 0:N], ACT.Copy).then_inc(xh_ready, 1)
            for n in range(SPLIT):
                split_high(act, n)
            act.wait_ge(nat_T, 3)
            for i in range(2):
                act.activation(taps[:, 12 * i:12 * i + 12, :],
                               bank[4 + i][:, 0:336].rearrange("p (t c) -> p t c", c=28), ACT.Copy).then_inc(taps_ready, 1)
            act.activation(vecs[:, :, :], bank[6][:, 0:216].rearrange("p (t c) -> p t c", c=27), ACT.Copy)\
                .then_inc(taps_ready, 1)
            act.wait_ge(gate_a, 1)
            step(act.activation(sp[1][:, :], sp[1][:, :], ACT.Exp, scale=-1.0))
            act.wait_ge(small_in, 80)
            step(act.activation(a_log[:, :], a_log[:, :], ACT.Exp))
            step.wait()
            act.activation(sp[1][:, :], sp[1][:, :], ACT.Ln, bias=1.0).then_inc(gate_b, 1)
            act.wait_ge(ab_psum, 2)
            act.activation(beta[:, :], bank[6][0:8, 0:N], ACT.Sigmoid).then_inc(gate_b, 1)
            for i in range(4):
                act.dma_start(s0a[:, i, :, :], state_gdn_S[0, i].rearrange("h k v -> k h v")).then_inc(s0a_in, 16)
            act.wait_ge(const_ready, 5)

            def inverse_norm(g):
                for t in range(4):
                    act.wait_ge(sq_psum, 4 * g + t + 1)
                    act.activation(squares[:, g % 2, t, :], bank[4 + t][:, 0:N], ACT.Ln, bias=eps[:, 0:1]).then_inc(sq_log, 1)
                act.wait_ge(sq_log, 4 * g + 4)
                act.activation(squares[:, g % 2, :, :], squares[:, g % 2, :, :], ACT.Exp, scale=-0.5).then_inc(sq_inv, 1)

            for n in range(OUT0):
                act.wait_ge(slot_used, n + 1)
                for t in range(2):
                    f = 2 * n + t
                    src = bank[2 * (n % 2) + t][:, 0:N]
                    if f < QT:
                        if f >= 4:
                            act.wait_ge(conv_done, f - 3)
                        act.activation(U[:, f % 4, TAPS - 1:], src, ACT.Copy).then_inc(proj_out, 1)
                    else:
                        act.activation(zgate[:, f - QT, :], src, ACT.Copy).then_inc(proj_out, 1)
                split_high(act, n + SPLIT)
                for t in range(2):
                    f = 2 * (n - 1) + t
                    if 0 <= f < QT:
                        act.wait_ge(conv_done, f + 1)
                        act.activation(qkv[:, f, 0:NP], qkv[:, f, 0:NP], ACT.Silu).then_inc(silu_done, 1)
                if n == 2:
                    act.wait_ge(gcol_psum, 1)
                    act.activation(aS[:, :, :], bank[5][:, 0:64].rearrange("p (h b) -> p h b", h=8), ACT.Exp).then_inc(aS_ready, 1)
                    act.wait_ge(gcol_ready, 1)
                    act.activation(nbe[:, :, :], gcol[:, :, 0, :], ACT.Exp).then_inc(nbe_ready, 1)
                if n == QT // 2:
                    act.wait_ge(conv_done, QT + 1)
                    act.activation(qkv[:, :, NP:N], qkv[:, :, NP:N], ACT.Silu).then_inc(silu_done, 1)
                    act.wait_ge(silu_done, QT + 1)
                if n >= QT // 2:
                    g = n - QT // 2
                    if g >= 2:
                        act.wait_ge(qk_ready, g - 1)
                    act.activation(squares[:, g % 2, :, :], qkv[:, 4 * g:4 * g + 4, :], ACT.Square).then_inc(sq_ready, 1)
                    if g:
                        inverse_norm(g - 1)
            inverse_norm(3)
            for i in range(6):
                act.wait_ge(tail_psum, i + 1)
                act.activation(tail_nat[:, 512 * i:512 * i + 512], bank[i % 4][0:11, :], ACT.Copy).then_inc(tail_sb, 1)
            act.wait_ge(qk_ready, 4)
            for i in range(4):
                act.dma_start(s0b[:, i, :, :], state_gdn_S[0, 4 + i].rearrange("h k v -> k h v")).then_inc(s0b_in, 16)
            act.wait_ge(proj_out, 2 * OUT0)
            act.activation(zgate[:, :, :], zgate[:, :, :], ACT.Silu).then_inc(z_ready, 1)
            act.wait_ge(dn_psum, 1)
            for i in range(2):
                act.activation(kn_s[:, 512 * i:512 * i + 512], bank[i][0:8, :], ACT.Copy).then_inc(kn_ready, 1)
            for c in range(NCH):
                act.wait_ge(bc_psum, c + 1)
                if c == 0:
                    act.wait_ge(sa_out, 64)
                for g in range(2):
                    hs = slice(4 * g, 4 * g + 4)
                    act.activation(gB[:, hs, :], heads(g), ACT.Copy).then_inc(g_act, 1)
                for g in range(2):
                    hs = slice(4 * g, 4 * g + 4)
                    act.activation(egB[:, hs, :], heads(g), ACT.Exp).then_inc(g_act, 1)
                act.wait_ge(d_ready, 2 * c + 1)
                act.activation(DM[:, :, :], DM[:, :, :], ACT.Exp).then_inc(e_ready, 1)
                act.wait_ge(d_ready, 2 * c + 2)
                act.activation(kd[:, c, :], kd[:, c, :], ACT.Exp).then_inc(e_ready, 1)
                act.wait_ge(nat_psum, c + 1)
                for g in range(2):
                    hs = slice(4 * g, 4 * g + 4)
                    act.activation(Kn[:, hs, :], heads(g), ACT.Copy).then_inc(kv_nat, 1)
                    act.activation(Vn[:, hs, :], heads(2 + g), ACT.Copy).then_inc(kv_nat, 1)
                for g in range(2):
                    hs = slice(4 * g, 4 * g + 4)
                    act.wait_ge(t1_psum, 2 * c + g + 1)
                    act.activation(T[:, hs, :], heads(6 + g), ACT.Copy).then_inc(p1_ready, 1)
                for s in range(1, LEVELS):
                    for g in range(2):
                        hs = slice(4 * g, 4 * g + 4)
                        act.wait_ge(p1_psum, 2 * (LEVELS - 1) * c + 2 * (s - 1) + g + 1)
                        act.activation(P1[:, hs, :], heads(3 * g), ACT.Copy).then_inc(p1_ready, 1)
                act.wait_ge(vn_psum, c + 1)
                for g in range(2):
                    hs = slice(4 * g, 4 * g + 4)
                    act.activation(P1[:, hs, :], heads(2 + g), ACT.Copy).then_inc(vn_ready, 1)
                act.wait_ge(oS_psum, c + 1)
                for g in range(2):
                    hs = slice(16 + 4 * g, 16 + 4 * g + 4)
                    act.activation(qkv[:, hs, CH * c:CH * c + CH], heads(4 + g), ACT.Copy).then_inc(o_ready, 1)
            act.wait_ge(o_ready, 2 * NCH)
            act.wait_ge(delta_ready, 1)
            for k in range(KT):
                act.activation(osq[:, k, :], qkv[:, 16 + k, :], ACT.Square).then_inc(osq_ready, 1)
            for k in range(KT):
                act.wait_ge(osq_psum, k + 1)
                act.activation(osq[:, k, :], bank[k][:, 0:N], ACT.Ln, scale=1.0 / 128, bias=eps[:, 0:1]).then_inc(o_inv, 1)
            for k in range(KT):
                act.wait_ge(o_inv, k + 1)
                act.activation(osq[:, k, :], osq[:, k, :], ACT.Exp, scale=-0.5).then_inc(o_root, 1)
            for k in range(KT):
                act.wait_ge(on_ready, k + 1)
                act.activation(xh[:, k, :], qkv[:, 16 + k, :], ACT.Copy).then_inc(xh_ready, 1)
            for n in range(OUT0, GU0):
                act.wait_ge(slot_used, n + 1)
                split_high(act, n + SPLIT)

            def layer_norm(l, split):
                for k in range(KT):
                    act.wait_ge(xc_ready, 8 * l + k + 1)
                    act.activation(lnsq[:, k, :], xres[:, k, :], ACT.Square).then_inc(lnsq_ready, 1)
                act.wait_ge(var_psum, l + 1)
                act.activation(rvar[:, :], bank[5][:, 0:N], ACT.Ln, scale=1.0 / D, bias=eps[:, 1:2]).then_inc(var_inv, 1)
                act.wait_ge(var_inv, l + 1)
                act.activation(rstd[:, :], rvar[:, :], ACT.Exp, scale=-0.5).then_inc(var_root, 1)
                for k in range(KT):
                    act.wait_ge(scaled, 8 * l + k + 1)
                    act.activation(xres[:, k, :], xres[:, k, :], ACT.Identity, bias=vecs[:, k, 4 + l:5 + l])\
                        .then_inc(x_new, 1)
                    if split:
                        if k:
                            act.wait_ge(x_new, 8 * l + k)
                            act.activation(xh[:, k - 1, :], xres[:, k - 1, :], ACT.Copy).then_inc(xh_ready, 1)
                if split:
                    act.wait_ge(x_new, 8 * l + 8)
                    act.activation(xh[:, KT - 1, :], xres[:, KT - 1, :], ACT.Copy).then_inc(xh_ready, 1)

            layer_norm(0, True)
            act.wait_ge(hist_out, 48)
            for i in range(FF // 256):
                n = GU0 + 2 * i
                act.wait_ge(slot_used, n + 1)
                for t in range(2):
                    if i >= 2:
                        act.wait_ge(h_ready, 2 * (i - 2) + t + 1)
                    act.activation(sg[:, 2 * (i % 2) + t, :], bank[4 * (i % 2) + t][:, 0:N], ACT.Silu).then_inc(gate_silu, 1)
                split_high(act, n + SPLIT)
                for t in range(2):
                    act.wait_ge(h_ready, 2 * i + t + 1)
                    act.activation(hh[:, 2 * i + t, :], hf[:, 2 * (i % 2) + t, :], ACT.Copy).then_inc(hh_ready, 1)
                split_high(act, n + 1 + SPLIT)
            for n in range(DOWN0, SCI0):
                act.wait_ge(slot_used, n + 1)
                split_high(act, n + SPLIT)
            layer_norm(1, True)
            for i in range(D // 256):
                n = SCI0 + 2 * i
                act.wait_ge(slot_used, n + 1)
                for t in range(2):
                    if i >= 2:
                        act.wait_ge(u_ready, 2 * (i - 2) + t + 1)
                    act.activation(cc[:, 2 * (i % 2) + t, :], bank[4 * (i % 2) + t][:, 0:N], ACT.Copy).then_inc(c_copied, 1)
                split_high(act, n + SPLIT)
                act.wait_ge(slot_used, n + 2)
                split_high(act, n + 1 + SPLIT)
            for i in range(D // 256):
                n = SCI0 + 2 * D // 256 + i
                for t in range(2):
                    act.wait_ge(sy_ready, 2 * i + t + 1)
                    act.activation(yh[:, 2 * i + t, :], sy[:, 2 * (i % 2) + t, :], ACT.Copy).then_inc(yh_ready, 1)
                split_high(act, n + SPLIT)
            for i in range(2):
                act.wait_ge(stail_psum, i + 1)
                act.activation(stail_nat[:, 512 * i:512 * i + 512], bank[4 + i][0:10, :], ACT.Copy).then_inc(stail_sb, 1)
            for n in range(SCO0, MOE0):
                act.wait_ge(slot_used, n + 1)
                if n + SPLIT < MOE0:
                    split_high(act, n + SPLIT)
            layer_norm(2, False)
            for i in range(6):
                act.wait_ge(xn_psum, i + 1)
                p = 128 if i < 4 else 8
                act.wait_ge(pool_step, 3 + 2 * LEVELS + 8)
                act.activation(xnh[0:p, i // 2, 512 * (i % 2):512 * (i % 2) + 512], bank[i][0:p, :], ACT.Copy)\
                    .then_inc(xnh_ready, 1)
            act.wait_ge(top_ready, 1)
            act.activation(gates[:, :, :], gates[:, :, :], ACT.Exp).then_inc(ex_ready, 1)

            def gathered(jobs):
                for g in range(2):
                    act.wait_ge(xg_psum, jobs * 4 + (g + 1))
                    act.activation(xgh[:, 4 * g:4 * g + 4, :], heads(g), ACT.Copy).then_inc(xgh_ready, 1)

            gathered(0)
            act.wait_ge(tiles_ready, 1)
            tiles = act.value_load(tiles_i[0:1, 0:1], min_val=1, max_val=TILES)
            with act.Fori(0, tiles) as t:
                with act.Fori(0, EX) as e:
                    job = t * EX + e
                    done, rounds = job * EXPERT_SLOTS, job * (16 * EXPERT_SLOTS // RAW)
                    units = job * UNITS
                    for i in range(SPLIT):
                        split_high(act, MOE0 + i, done, rounds)

                    def hidden_T(u):
                        act.wait_ge(ht_psum, units + (u + 1))
                        act.activation(hth[:, u % 2, :], bank[6][:, :], ACT.Copy).then_inc(hth_ready, 1)

                    for i in range(EXPERT_SLOTS):
                        for u in range(UNITS):
                            if i == unit_first(u) + 1:
                                act.wait_ge(slot_used, done + (MOE0 + i + 1))
                                act.activation(sgx[:, u % 2, :], bank[2 * (u % 2)][:, :], ACT.Silu).then_inc(sgx_ready, 1)
                                if u:
                                    hidden_T(u - 1)
                        if i == unit_first(0) + 3:
                            act.wait_ge(pt_psum, job + 1)
                            act.activation(pth[:, :], bank[7][:, 0:N], ACT.Copy).then_inc(pth_ready, 1)
                        if i == EXPERT_SLOTS - 3:
                            hidden_T(UNITS - 1)
                            gathered(job + 1)
                        if i == EXPERT_SLOTS - 1:
                            act.wait_ge(slot_used, done + (MOE0 + i + 1))
                            for g in range(2):
                                act.activation(yxh[:, 512 * g:512 * g + 512], bank[4 + g][:, :], ACT.Copy)\
                                    .then_inc(yxh_ready, 1)
                        if i + SPLIT < EXPERT_SLOTS:
                            split_high(act, MOE0 + i + SPLIT, done, rounds)
            layer_norm(3, False)
            for i in range(6):
                act.wait_ge(y_psum, i + 1)
                p = 128 if i < 4 else 8
                act.activation(ynat[0:p, i // 2, 512 * (i % 2):512 * (i % 2) + 512], bank[i][0:p, :], ACT.Copy)\
                    .then_inc(y_sb, 1)

        @block.vector
        def _(dve):
            step = Steps(dve, dve_step)
            for k in range(KT):
                dve.wait_ge(xh_ready, k + 1)
                step(dve.tensor_copy(xres[:, k, :], bank[k][:, 0:N]))
                dve.tensor_tensor(xl[:, k, :], bank[k][:, 0:N], xh[:, k, :].bitcast(F32), ALU.subtract).then_inc(xl_ready, 1)
            for n in range(SPLIT):
                split_low(dve, n)
            dve.wait_ge(ab_psum, 1)
            dve.wait_ge(small_in, 80)
            step(dve.tensor_scalar(sp[0][:, :], bank[7][0:8, 0:N], dt_bias[:, 0:1], None, ALU.add))
            step.wait()
            dve.scalar_tensor_tensor(sp[1][:, :], sp[0][:, :], -1.0, sp[0][:, :], ALU.mult, ALU.max).then_inc(gate_a, 1)
            dve.wait_ge(gate_b, 1)
            step(dve.scalar_tensor_tensor(sp[0][:, :], sp[0][:, :], 0.0, sp[1][:, :], ALU.max, ALU.add))
            step.wait()
            step(dve.tensor_scalar(sp[0][:, :], sp[0][:, :], a_log[:, 0:1], -1.0, ALU.mult, ALU.mult))
            step(dve.memset(sp[1][:, :], 1.0))
            step.wait()
            for c in range(NCH):
                cs = slice(CH * c, CH * c + CH)
                dve.tensor_tensor_scan(gg[:, cs], sp[1][:, cs], sp[0][:, cs], 0.0, ALU.mult, ALU.add).then_inc(gate_ready, 1)
            dve.tensor_copy(gg[:, NP:N], sp[0][:, NP:N]).then_inc(gate_ready, 1)

            def normalise(g):
                dve.wait_ge(sq_inv, g + 1)
                v = qkv[:, 4 * g:4 * g + 4, :]
                if g < 2:
                    dve.scalar_tensor_tensor(v, v, 128 ** -0.5, squares[:, g % 2, :, :], ALU.mult, ALU.mult).then_inc(qk_ready, 1)
                else:
                    dve.tensor_tensor(v, v, squares[:, g % 2, :, :], ALU.mult).then_inc(qk_ready, 1)

            for n in range(OUT0):
                fs = [f for f in (2 * n, 2 * n + 1) if f < QT]
                if fs:
                    if n == 0:
                        dve.wait_ge(taps_ready, 2)
                    dve.wait_ge(proj_out, fs[-1] + 1)
                    for j in range(TAPS):
                        if j:
                            step.wait()
                        for f in fs:
                            u, w = U[:, f % 4, j:j + NP], taps[:, f, 24 + j:25 + j]
                            o = qkv[:, f, 0:NP]
                            if j == 0:
                                step(dve.tensor_scalar(o, u, w, None, ALU.mult))
                            else:
                                step(dve.scalar_tensor_tensor(o, u, w, o, ALU.mult, ALU.add))
                    for f in fs:
                        dve.tensor_copy(utail[:, f, :], U[:, f % 4, NP:NP + 11]).then_inc(conv_done, 1)
                split_low(dve, n + SPLIT)
                if n == 2:
                    dve.wait_ge(gcol_psum, 1)
                    step(dve.tensor_copy(bS[:, :, :], bank[6][:, 0:64].rearrange("p (h b) -> p h b", h=8)))
                    dve.tensor_copy(gcol[:, :, :, :], bank[4][:, 0:32].rearrange("p (c a h) -> p c a h", c=2, a=2)).then_inc(gcol_ready, 1)
                    dve.wait_ge(nbe_ready, 1)
                    step(dve.scalar_tensor_tensor(nbe[:, :, :], nbe[:, :, :], -1.0, gcol[:, :, 1, :], ALU.mult, ALU.mult))
                if n == QT // 2 - 1:
                    new, tmp = qkv[:, :, NP:N], sconv_tmp[:, :, :]
                    dve.wait_ge(conv_done, QT)
                    for j in range(TAPS):
                        row = taps[:, :, 8 * j:8 * j + 8] if j < TAPS - 1 else utail[:, :, 3:11]
                        w = taps[:, :, 24 + j:25 + j].to_broadcast([128, QT, NS])
                        step(dve.tensor_tensor(tmp if j else new, row, w, ALU.mult))
                        step.wait()
                        if j:
                            ins = dve.tensor_tensor(new, new, tmp, ALU.add)
                            if j < TAPS - 1:
                                step(ins)
                                step.wait()
                            else:
                                ins.then_inc(conv_done, 1)
                if n >= QT // 2 + 2:
                    normalise(n - QT // 2 - 2)
            normalise(2)
            normalise(3)
            dve.wait_ge(qk_ready, 4)
            dve.tensor_tensor(kq[:, :, :], qkv[:, 0:8, NP:N], qkv[:, 8:16, NP:N], ALU.mult).then_inc(kq_ready, 1)
            dve.wait_ge(dec_psum, 3)
            dve.wait_ge(aS_ready, 1)
            dec = bank[7][:, 0:128].rearrange("p (b h two) -> p h b two", b=8, two=2)
            step(dve.tensor_tensor(tmpS[:, :, :], dec[:, :, :, 1], aS[:, :, :], ALU.mult))
            step.wait()
            step(dve.tensor_tensor(tmpS[:, :, :], qkv[:, 16:24, NP:N], tmpS[:, :, :], ALU.subtract))
            step.wait()
            step(dve.tensor_tensor(delta[:, :, :], tmpS[:, :, :], bS[:, :, :], ALU.mult))
            step.wait()
            step(dve.tensor_tensor(qkv[:, 16:24, NP:N], dec[:, :, :, 0], aS[:, :, :], ALU.mult))
            step(dve.tensor_tensor(tmpS[:, :, :], bank[5][:, 0:64].rearrange("p (h b) -> p h b", h=8), delta[:, :, :], ALU.mult))
            step.wait()
            dve.tensor_tensor(qkv[:, 16:24, NP:N], qkv[:, 16:24, NP:N], tmpS[:, :, :], ALU.add).then_inc(delta_ready, 1)
            dve.wait_ge(dn_psum, 2)

            def mask_delta(i):
                h, half = i % HEADS, i // HEADS
                if i >= 2:
                    dve.wait_ge(outer_psum, i - 1)
                dn = bank[2 + h // 4][0:8, 128 * (h % 4):128 * (h % 4) + 128]
                dve.tensor_tensor(dmask[:, i % 2, :, :], dn.rearrange("p (o v) -> p o v", o=1).to_broadcast([8, 4, 128]),
                                  ident[0:8, 4 * half:4 * half + 4].rearrange("p (b o) -> p b o", o=1).to_broadcast([8, 4, 128]),
                                  ALU.mult).then_inc(dmask_ready, 1)

            mask_delta(0)
            for i in range(2 * HEADS):
                if i + 1 < 2 * HEADS:
                    mask_delta(i + 1)
                h, half, s0 = i % HEADS, i // HEADS, (s0a, s0b)[i // HEADS]
                dve.wait_ge(outer_psum, i + 1)
                for b in range(4):
                    ins = dve.scalar_tensor_tensor(s0[:, b, h, :], s0[:, b, h, :], aS[:, h, 4 * half + b:4 * half + b + 1],
                                                   heads(4 + i % 4)[:, b, :], ALU.mult, ALU.add)
                    if b < 3:
                        step(ins)
                ins.then_inc(s_updated, 1)
            for c in range(NCH):
                cs = slice(CH * c, CH * c + CH)
                dve.wait_ge(bc_psum, c + 1)
                if c == 0:
                    dve.wait_ge(sa_out, 64)
                for g in range(2):
                    dve.tensor_copy(bB[:, 4 * g:4 * g + 4, :], heads(2 + g)).then_inc(b_dve, 1)
                dve.wait_ge(g_act, 4 * c + 2)
                if c == 0:
                    dve.wait_ge(tail_out, 32)
                else:
                    dve.wait_ge(oS_psum, c)
                for h in range(HEADS):
                    ins = dve.tensor_scalar(DM[:, h, :], gB[:, h, :], gcol[:, c, 0, h:h + 1], 0.0, ALU.subtract, ALU.min)
                    if h < HEADS - 1:
                        step(ins)
                ins.then_inc(d_ready, 1)
                dve.tensor_tensor(kd[:, c, :], gB[:, :, CH - 1], gcol[:, c, 0, :], ALU.subtract).then_inc(d_ready, 1)
                dve.wait_ge(e_ready, 2 * c + 1)
                if c == 0:
                    dve.wait_ge(mask_ready, 1)
                step(dve.tensor_tensor(DM[:, :, :], DM[:, :, :],
                                       upper[:, :].rearrange("p (o i) -> p o i", o=1).to_broadcast([128, 8, CH]), ALU.mult))
                step.wait()
                dve.wait_ge(kk_psum, c + 1)
                for g in range(2):
                    hs = slice(4 * g, 4 * g + 4)
                    step(dve.tensor_tensor(AT[:, hs, :], heads(4 + g), DM[:, hs, :], ALU.mult))
                    step.wait()
                    dve.tensor_tensor(AT[:, hs, :], AT[:, hs, :], bB[:, hs, :], ALU.mult).then_inc(at_ready, 1)
                for g in range(2):
                    hs = slice(4 * g, 4 * g + 4)
                    step(dve.tensor_tensor(DM[:, hs, :], heads(6 + g), DM[:, hs, :], ALU.mult))
                dve.wait_ge(g_act, 4 * c + 4)
                step(dve.tensor_tensor(qkv[:, 0:8, cs], qkv[:, 0:8, cs], egB[:, :, :], ALU.mult))
                if c:
                    dve.wait_ge(vn_psum, c)
                for g in range(2):
                    hs = slice(4 * g, 4 * g + 4)
                    dve.wait_ge(atm_ready, 2 * LEVELS * c + g + 1)
                    dve.tensor_tensor(TT[:, hs, :], ident[:, :].rearrange("p (o i) -> p o i", o=1).to_broadcast([128, 4, CH]),
                                      ATm[:, hs, :], ALU.subtract).then_inc(tt1_ready, 1)
                dve.wait_ge(kv_nat, 4 * (c + 1))
                dve.wait_ge(e_ready, 2 * c + 2)
                step(dve.tensor_tensor(Kn[:, :, :], Kn[:, :, :],
                                       kd[:, c, :].rearrange("p (h o) -> p h o", o=1).to_broadcast([128, 8, 128]), ALU.mult))
                ins = dve.tensor_tensor(Vn[:, :, :], Vn[:, :, :],
                                        gcol[:, c, 1, :].rearrange("p (h o) -> p h o", o=1).to_broadcast([128, 8, 128]), ALU.mult)
                if c == 0:
                    ins.then_inc(r_ready, 1)
                else:
                    step(ins)
                for s in range(1, LEVELS):
                    for g in range(2):
                        hs = slice(4 * g, 4 * g + 4)
                        dve.wait_ge(dd_psum, 2 * (LEVELS - 1) * c + 2 * (s - 1) + g + 1)
                        if s < LEVELS - 1:
                            step(dve.tensor_tensor(T[:, hs, :], T[:, hs, :], heads(3 * g + 1), ALU.subtract))
                        dve.tensor_tensor(TT[:, hs, :], TT[:, hs, :], heads(3 * g + 2), ALU.subtract).then_inc(t_ready, 1)
                if c:
                    dve.wait_ge(ks_psum, c)
                    for g in range(2):
                        hs = slice(4 * g, 4 * g + 4)
                        step(dve.tensor_tensor(ATm[:, hs, :], heads(g),
                                               nbe[:, c, hs].rearrange("p (h o) -> p h o", o=1).to_broadcast([128, 4, 128]),
                                               ALU.mult))
                    step.wait()
                    dve.tensor_tensor(Vn[:, :, :], Vn[:, :, :], ATm[:, :, :], ALU.add).then_inc(r_ready, 1)
                if c:
                    dve.wait_ge(oS_psum, c + 1)
                    step(dve.tensor_tensor(S[:, :, :], S[:, :, :], egB[:, :, CH - 1:CH].to_broadcast([128, 8, 128]), ALU.mult))
                    step.wait()
                    for g in range(2):
                        hs = slice(4 * g, 4 * g + 4)
                        dve.tensor_tensor(S[:, hs, :], S[:, hs, :], heads(6 + g), ALU.add).then_inc(s_ready, 1)
                else:
                    dve.wait_ge(oS_psum, c + 1)
                    for g in range(2):
                        dve.tensor_copy(S[:, 4 * g:4 * g + 4, :], heads(6 + g)).then_inc(s_ready, 1)
            for k in range(KT):
                dve.wait_ge(o_root, k + 1)
                step(dve.scalar_tensor_tensor(qkv[:, 16 + k, :], qkv[:, 16 + k, :], norm_w[:, 0:1], osq[:, k, :],
                                              ALU.mult, ALU.mult))
            step.wait()
            dve.wait_ge(z_ready, 1)
            for k in range(KT):
                dve.tensor_tensor(qkv[:, 16 + k, :], qkv[:, 16 + k, :], zgate[:, k, :], ALU.mult).then_inc(on_ready, 1)
            for k in range(KT):
                dve.wait_ge(xh_ready, 8 + k + 1)
                dve.tensor_tensor(xl[:, k, :], qkv[:, 16 + k, :], xh[:, k, :].bitcast(F32), ALU.subtract).then_inc(xl_ready, 1)

            def add_residual(d, b):
                dve.scalar_tensor_tensor(xres[:, d, :], xres[:, d, :], ALPHA, bank[b][:, 0:N], ALU.mult, ALU.add)\
                    .then_inc(res_ready, 1)

            for n in range(OUT0, GU0):
                dve.wait_ge(slot_used, n + 1)
                for t in range(2):
                    add_residual(2 * (n - OUT0) + t, 2 * (n % 2) + t)
                split_low(dve, n + SPLIT)

            def layer_norm(l, split):
                dve.wait_ge(mean_psum, l + 1)
                step(dve.tensor_scalar(mu[:, :], bank[4][:, 0:N], 1.0 / D, None, ALU.mult))
                step.wait()
                for k in range(KT):
                    dve.tensor_tensor(xres[:, k, :], xres[:, k, :], mu[:, :], ALU.subtract).then_inc(xc_ready, 1)
                dve.wait_ge(var_root, l + 1)
                for k in range(KT):
                    dve.scalar_tensor_tensor(xres[:, k, :], xres[:, k, :], vecs[:, k, l:l + 1], rstd[:, :],
                                             ALU.mult, ALU.mult).then_inc(scaled, 1)
                if split:
                    for k in range(KT):
                        dve.wait_ge(xh_ready, 8 * (l + 2) + k + 1)
                        dve.tensor_tensor(xl[:, k, :], xres[:, k, :], xh[:, k, :].bitcast(F32), ALU.subtract)\
                            .then_inc(xl_ready, 1)

            layer_norm(0, True)
            for i in range(FF // 256):
                n = GU0 + 2 * i
                dve.wait_ge(slot_used, n + 1)
                split_low(dve, n + SPLIT)
                dve.wait_ge(slot_used, n + 2)
                dve.wait_ge(gate_silu, 2 * i + 2)
                for t in range(2):
                    if i >= 2:
                        dve.wait_ge(hl_ready, 2 * (i - 2) + t + 1)
                    r = 2 * (i % 2) + t
                    dve.tensor_tensor(hf[:, r, :], sg[:, r, :], bank[4 * (i % 2) + 2 + t][:, 0:N], ALU.mult).then_inc(h_ready, 1)
                for t in range(2):
                    dve.wait_ge(hh_ready, 2 * i + t + 1)
                    dve.tensor_tensor(hl[:, 2 * i + t, :], hf[:, 2 * (i % 2) + t, :], hh[:, 2 * i + t, :].bitcast(F32),
                                      ALU.subtract).then_inc(hl_ready, 1)
                split_low(dve, n + 1 + SPLIT)
            for n in range(DOWN0, SCI0):
                dve.wait_ge(slot_used, n + 1)
                if n == SCI0 - 1:
                    for d in range(KT):
                        add_residual(d, d)
                split_low(dve, n + SPLIT)
            layer_norm(1, True)
            dve.wait_ge(const_ready, 6)
            for i in range(D // 256):
                n = SCI0 + 2 * i
                dve.wait_ge(slot_used, n + 1)
                split_low(dve, n + SPLIT)
                dve.wait_ge(slot_used, n + 2)
                dve.wait_ge(c_copied, 2 * i + 2)
                for t in range(2):
                    f = 2 * i + t
                    dve.tensor_tensor(su[:, f, SCW - 1:], cc[:, 2 * (i % 2) + t, :], bank[4 * (i % 2) + 2 + t][:, 0:N],
                                      ALU.mult).then_inc(u_ready, 1)
                dve.wait_ge(u_ready, 2 * i + 2)
                for j in range(SCW):
                    if j:
                        step.wait()
                    for t in range(2):
                        f = 2 * i + t
                        u, w, o = su[:, f, j:j + NP], vecs[:, f, 8 + j:9 + j], sc[:, f, 0:NP]
                        if j == 0:
                            step(dve.tensor_scalar(o, u, w, None, ALU.mult))
                        else:
                            step(dve.scalar_tensor_tensor(o, u, w, o, ALU.mult, ALU.add))
                split_low(dve, n + 1 + SPLIT)
            new, tmp = sc[:, :, NP:N], sconv_tmp[:, 0:KT, :]
            for j in range(SCW):
                row = vecs[:, :, 11 + 8 * j:19 + 8 * j] if j < SCW - 1 else su[:, :, SCW - 1 + NP:]
                w = vecs[:, :, 8 + j:9 + j].to_broadcast([128, KT, NS])
                step(dve.tensor_tensor(tmp if j else new, row, w, ALU.mult))
                step.wait()
                if j:
                    step(dve.tensor_tensor(new, new, tmp, ALU.add))
                    step.wait()
            for i in range(D // 256):
                n = SCI0 + 2 * D // 256 + i
                dve.wait_ge(slot_used, n + 1)
                for t in range(2):
                    f = 2 * i + t
                    if i >= 2:
                        dve.wait_ge(yl_ready, 2 * (i - 2) + t + 1)
                    dve.tensor_tensor(sy[:, 2 * (i % 2) + t, :], sc[:, f, :], bank[f][:, 0:N], ALU.mult).then_inc(sy_ready, 1)
                for t in range(2):
                    f = 2 * i + t
                    dve.wait_ge(yh_ready, f + 1)
                    dve.tensor_tensor(yl[:, f, :], sy[:, 2 * (i % 2) + t, :], yh[:, f, :].bitcast(F32), ALU.subtract)\
                        .then_inc(yl_ready, 1)
                split_low(dve, n + SPLIT)
            for n in range(SCO0, MOE0):
                dve.wait_ge(slot_used, n + 1)
                for t in range(2):
                    add_residual(2 * (n - SCO0) + t, 2 * ((n - SCO0) % 2) + t)
                if n + SPLIT < MOE0:
                    split_low(dve, n + SPLIT)
            layer_norm(2, False)
            for i in range(6):
                dve.wait_ge(xnh_ready, i + 1)
                p, cs = (128 if i < 4 else 8), slice(512 * (i % 2), 512 * (i % 2) + 512)
                dve.tensor_tensor(xnl[0:p, i // 2, cs], bank[i][0:p, :], xnh[0:p, i // 2, cs].bitcast(F32),
                                  ALU.subtract).then_inc(xnl_ready, 1)
            dve.wait_ge(logit_psum, 1)
            dve.wait_ge(const_ready, 7)
            step(dve.tensor_copy(logits[:, 0:2, :], bank[6][:, 0:16].rearrange("p (t e) -> p t e", t=2)))
            step(dve.tensor_copy(logits[0:8, 2, :], bank[6][0:8, 16:24]))
            step.wait()
            step(dve.tensor_reduce(top[:, :], logits[:, :, :], X, ALU.max))
            for tt in range(3):
                mine = logits[:, tt, :].rearrange("p (e o) -> p e o", o=1).to_broadcast([128, EX, EX])
                other = logits[:, tt, :].rearrange("p (o e) -> p o e", o=1).to_broadcast([128, EX, EX])
                step(dve.tensor_tensor(cmp_gt[:, tt, :, :], other, mine, ALU.is_gt))
                step(dve.tensor_tensor(cmp_eq[:, tt, :, :], other, mine, ALU.is_equal))
            step.wait()
            dve.tensor_tensor(gates[:, :, :], logits[:, :, :], top[:, :].rearrange("p (t o) -> p t o", o=1)
                              .to_broadcast([128, 3, EX]), ALU.subtract).then_inc(top_ready, 1)
            for tt in range(3):
                step(dve.tensor_tensor(cmp_eq[:, tt, :, :], cmp_eq[:, tt, :, :], before[:, :, :], ALU.mult))
            step.wait()
            step(dve.tensor_tensor(cmp_gt[:, :, :, :], cmp_gt[:, :, :, :], cmp_eq[:, :, :, :], ALU.add))
            step.wait()
            step(dve.tensor_reduce(rank[:, :, :], cmp_gt[:, :, :, :], X, ALU.add))
            step.wait()
            step(dve.tensor_scalar(sel[:, :, :], rank[:, :, :], 1.5, None, ALU.is_lt))
            step.wait()
            dve.tensor_tensor(sel[:, :, :], sel[:, :, :], valid[:, :, :], ALU.mult).then_inc(sel_ready, 1)
            dve.wait_ge(sel_ready, 1)
            dve.wait_ge(ex_ready, 1)
            step(dve.tensor_tensor(gates[:, :, :], gates[:, :, :], sel[:, :, :], ALU.mult))
            step.wait()
            step(dve.tensor_reduce(top[:, :], gates[:, :, :], X, ALU.add))
            step.wait()
            step(dve.tensor_scalar(top[:, :], top[:, :], 1e-30, None, ALU.max))
            step.wait()
            step(dve.reciprocal(top[:, :], top[:, :]))
            step.wait()
            step(dve.tensor_tensor(gates[:, :, :], gates[:, :, :], top[:, :].rearrange("p (t o) -> p t o", o=1)
                                   .to_broadcast([128, 3, EX]), ALU.mult))
            dve.wait_ge(rank_psum, 1)
            step(dve.tensor_copy(rank[:, :, :], bank[7][:, 0:24].rearrange("p (t e) -> p t e", t=3)))
            step(dve.tensor_copy(total[:, :], bank[7][:, 24:32]))
            step.wait()
            step(dve.tensor_tensor(rank[:, :, :], rank[:, :, :], sel[:, :, :], ALU.mult))
            step(dve.tensor_reduce(most[:, 0:1], total[:, :], X, ALU.max))
            step.wait()
            for t in range(TILES):
                js = slice(EX * t, EX * t + EX)
                step(dve.tensor_scalar(slot_tab[:, js, :].rearrange("p e t -> p t e"), rank[:, :, :],
                                       -1.0 - CAP * t, None, ALU.add))
                step(dve.tensor_copy(gate_tab[:, js, :].rearrange("p e t -> p t e"), gates[:, :, :]))
            step(dve.tensor_scalar(most[:, 1:2], most[:, 0:1], float(CAP), 1.0, ALU.is_gt, ALU.add))
            step(dve.tensor_scalar(most[:, 2:3], most[:, 0:1], float(2 * CAP), None, ALU.is_gt))
            step.wait()
            dve.tensor_tensor(tiles_i[0:1, 0:1], most[0:1, 1:2], most[0:1, 2:3], ALU.add).then_inc(tiles_ready, 1)
            for k in range(KT):
                ins = dve.tensor_scalar(xres[:, k, :], xres[:, k, :], ALPHA, None, ALU.mult)
                if k < KT - 1:
                    step(ins)
            ins.then_inc(scat_done, 1)
            dve.wait_ge(scat_done, 1)

            def choose(table, to, at):
                return dve.tensor_copy(to, table[:, bass.ds(at, 1), :].rearrange("p a t -> p (a t)"))

            def pick_tokens(own):
                for tt in range(3):
                    ins = dve.tensor_scalar(pick[:, tt, :], iota_f[:, :], scol[:, tt:tt + 1], None, ALU.is_equal)
                    if tt < 2:
                        own(ins)
                ins.then_inc(pick_ready, 1)

            def gathered(jobs):
                for g in range(2):
                    dve.wait_ge(xg_psum, jobs * 4 + (g + 3))
                    dve.tensor_copy(xgl[:, 4 * g:4 * g + 4, :], heads(2 + g)).then_inc(xgl_ready, 1)

            step(dve.tensor_copy(scol[:, :], slot_tab[:, 0, :]))
            step.wait()
            pick_tokens(step)
            gathered(0)
            tiles = dve.value_load(tiles_i[0:1, 0:1], min_val=1, max_val=TILES)
            PER_JOB = 8
            with dve.Fori(0, tiles) as t:
                with dve.Fori(0, EX) as e:
                    job = t * EX + e
                    done, units = job * EXPERT_SLOTS, job * UNITS
                    own = Steps(dve, moe_step, job * PER_JOB)
                    for i in range(SPLIT):
                        split_low(dve, MOE0 + i, done)

                    def hidden_T(u):
                        dve.wait_ge(hth_ready, units + (u + 1))
                        dve.tensor_tensor(htl[:, u % 2, :], bank[6][:, :], hth[:, u % 2, :].bitcast(F32),
                                          ALU.subtract).then_inc(htl_ready, 1)

                    for i in range(EXPERT_SLOTS):
                        if i == 0:
                            own(choose(slot_tab, scol_g[:, :], job))
                            own(choose(gate_tab, gcol_g[:, :], job))
                            own(choose(slot_tab, scol[:, :], job + 1))
                            own.wait()
                            for tt in range(3):
                                ins = dve.tensor_scalar(pickg[:, tt, :], iota_f[:, :], scol_g[:, tt:tt + 1],
                                                        gcol_g[:, tt:tt + 1], ALU.is_equal, ALU.mult)
                                if tt < 2:
                                    own(ins)
                            ins.then_inc(pickg_ready, 1)
                            pick_tokens(own)
                        for u in range(UNITS):
                            if i == unit_first(u) + 1 and u:
                                hidden_T(u - 1)
                            if i == unit_first(u) + 3:
                                dve.wait_ge(slot_used, done + (MOE0 + i + 1))
                                dve.wait_ge(sgx_ready, units + (u + 1))
                                dve.tensor_tensor(hx[:, u % 2, :], sgx[:, u % 2, :], bank[2 * (u % 2) + 1][:, :],
                                                  ALU.mult).then_inc(hx_ready, 1)
                        if i == unit_first(0) + 3:
                            dve.wait_ge(pth_ready, job + 1)
                            dve.tensor_tensor(ptl[:, :], bank[7][:, 0:N], pth[:, :].bitcast(F32), ALU.subtract)\
                                .then_inc(ptl_ready, 1)
                        if i == EXPERT_SLOTS - 3:
                            hidden_T(UNITS - 1)
                            gathered(job + 1)
                        if i == EXPERT_SLOTS - 1:
                            for g in range(2):
                                dve.wait_ge(yxh_ready, job * 2 + (g + 1))
                                ys = slice(512 * g, 512 * g + 512)
                                dve.tensor_tensor(yxl[:, ys], bank[4 + g][:, :], yxh[:, ys].bitcast(F32),
                                                  ALU.subtract).then_inc(yxl_ready, 1)
                            for d in range(KT):
                                dve.wait_ge(scat_psum, job * KT + (d + 1))
                                dve.tensor_tensor(xres[:, d, :], xres[:, d, :], bank[6 + d % 2][:, 0:N], ALU.add)\
                                    .then_inc(scat_done, 1)
                        if i + SPLIT < EXPERT_SLOTS:
                            split_low(dve, MOE0 + i + SPLIT, done)
                    own(dve.memset(most[:, 3:4], 0.0))
                    assert own.count == PER_JOB, own.count
            dve.wait_ge(scat_done, tiles * (EX * KT) + 1)
            layer_norm(3, False)

        @block.tensor
        def _(pe):
            pe.wait_ge(const_ready, 5)
            pe.wait_ge(x_in, 32)
            idn = ident[:, :]
            for k in range(KT):
                ks = slice(128 * k, 128 * k + 128)
                for c in range(2):
                    pe.transpose(bank[k][:, 128 * c:128 * c + 128], xnat[:, c, ks], idn)
                pe.transpose(bank[k][:, NP:N], xsnat[:, ks], ident[0:8, 0:8]).then_inc(xT_psum, 1)
            pe.wait_ge(nat_in, 16 * 9)
            for i in range(2):
                pe.wait_ge(xl_ready, 5 + i)
                for t in range(12):
                    f = 12 * i + t
                    last = pe.transpose(bank[4 + i][:, 28 * t:28 * t + 28], taps_nat[:, 128 * f:128 * f + 128], ident[0:28, 0:28])
                last.then_inc(nat_T, 1)
            pe.wait_ge(xl_ready, 8)
            for k in range(KT):
                last = pe.transpose(bank[6][:, 27 * k:27 * k + 27], vecs_nat[:, 128 * k:128 * k + 128], ident[0:27, 0:27])
            last.then_inc(nat_T, 1)
            pe.wait_ge(small_in, 80)
            for part in range(2):
                if part:
                    pe.wait_ge(taps_ready, 3)
                for k in range(KT):
                    last = pe.matmul(bank[7 - part][0:8, 0:N], wab[:, k, 8 * part:8 * part + 8], xres[:, k, :],
                                     start=k == 0, stop=k == KT - 1)
                last.then_inc(ab_psum, 1)

            def square_sums(g):
                pe.wait_ge(sq_ready, g + 1)
                for t in range(4):
                    if g:
                        pe.wait_ge(sq_log, 4 * (g - 1) + t + 1)
                    pe.matmul(bank[4 + t][:, 0:N], ones[:, :], squares[:, g % 2, t, :], start=True, stop=True).then_inc(sq_psum, 1)

            for n in range(OUT0):
                if n >= 2:
                    pe.wait_ge(proj_out, 2 * n - 2)
                dense_slot(pe, n, 2 * (n % 2), xh, xl)
                if n == 1:
                    pe.wait_ge(gate_ready, NCH + 1)
                    pe.wait_ge(gate_b, 2)
                    for c in range(NCH):
                        for a, src in enumerate((gg, beta)):
                            at = 16 * c + 8 * a
                            pe.transpose(bank[4][:, at:at + 8], src[:, CH * c:CH * c + CH], ident[0:8, 0:8])
                    for b, src in ((5, gg), (6, beta)):
                        for h in range(HEADS):
                            last = pe.matmul(bank[b][:, 8 * h:8 * h + 8], ident[0:8, h:h + 1].to_broadcast([8, 128]),
                                             src[:, NP:N], start=True, stop=True)
                    last.then_inc(gcol_psum, 1)
                if n > QT // 2:
                    if n == QT // 2 + 1:
                        pe.wait_ge(gcol_ready, 1)
                        pe.wait_ge(aS_ready, 1)
                    square_sums(n - QT // 2 - 1)
            square_sums(3)
            pe.wait_ge(proj_out, 2 * OUT0)
            for i in range(6):
                if i >= 4:
                    pe.wait_ge(tail_sb, i - 3)
                for t in range(4):
                    last = pe.transpose(bank[i % 4][0:11, 128 * t:128 * t + 128], utail[:, 4 * i + t, :], idn)
                last.then_inc(tail_psum, 1)
            pe.wait_ge(qk_ready, 4)
            pe.wait_ge(tail_sb, 6)
            for half, (s0, arrived) in enumerate(((s0a, s0a_in), (s0b, s0b_in))):
                pe.wait_ge(arrived, 64)
                for i in range(4):
                    b = 4 * half + i
                    for h in range(HEADS):
                        at = 2 * (HEADS * b + h)
                        last = pe.matmul(bank[7][:, at:at + 2], s0[:, i, h, :], qkv[:, h:h + 9:8, NP + b], start=True, stop=True)
                last.then_inc(dec_psum, 1)
            pe.wait_ge(kq_ready, 1)
            pe.matmul(bank[5][:, 0:64], ones[:, :], kq[:, :, :].rearrange("p h b -> p (h b)"), start=True, stop=True)\
                .then_inc(dec_psum, 1)
            for h in range(HEADS):
                last = pe.transpose(bank[h // 4][0:8, 128 * (h % 4):128 * (h % 4) + 128], qkv[:, 8 + h, NP:N], idn)
            last.then_inc(dn_psum, 1)
            pe.wait_ge(delta_ready, 1)
            for h in range(HEADS):
                last = pe.transpose(bank[2 + h // 4][0:8, 128 * (h % 4):128 * (h % 4) + 128], delta[:, h, :], idn)
            last.then_inc(dn_psum, 1)
            pe.wait_ge(kn_ready, 2)
            for i in range(2 * HEADS):
                h = i % HEADS
                pe.wait_ge(dmask_ready, i + 1)
                if i >= 4:
                    pe.wait_ge(s_updated, i - 3)
                pe.matmul(bank[4 + i % 4][:, :], kn_s[:, 128 * h:128 * h + 128],
                          dmask[:, i % 2, :, :].rearrange("p b v -> p (b v)"), start=True, stop=True).then_inc(outer_psum, 1)
            for c in range(NCH):
                cs = slice(CH * c, CH * c + CH)
                if c == 0:
                    pe.wait_ge(s_updated, 16)
                    pe.wait_ge(dmask_ready, 2 * HEADS)
                else:
                    pe.wait_ge(o_ready, 2 * c)
                    pe.wait_ge(vn_ready, 2 * c)
                    pe.wait_ge(s_ready, 2 * c)
                    pe.wait_ge(t_ready, 2 * (LEVELS - 1) * c)
                for a, src in enumerate((gg, beta)):
                    for h in range(HEADS):
                        last = pe.matmul(heads(2 * a + h // 4)[:, h % 4, :], ident[0:8, h:h + 1].to_broadcast([8, 128]),
                                         src[:, cs], start=True, stop=True)
                last.then_inc(bc_psum, 1)
                for b, f in ((4, 8), (6, 0)):
                    for h in range(HEADS):
                        last = pe.matmul(heads(b + h // 4)[:, h % 4, :], qkv[:, 8 + h, cs], qkv[:, f + h, cs],
                                         start=True, stop=True)
                last.then_inc(kk_psum, 1)
                pe.wait_ge(g_act, 4 * c + 4)
                pe.wait_ge(b_dve, 2 * c + 2)
                for b, f in ((0, 8), (2, 16)):
                    for h in range(HEADS):
                        last = pe.transpose(heads(b + h // 4)[:, h % 4, :], qkv[:, f + h, cs], idn)
                last.then_inc(nat_psum, 1)
                for g in range(2):
                    pe.wait_ge(tt1_ready, 2 * c + g + 1)
                    for h in range(4):
                        last = pe.transpose(heads(6 + g)[:, h, :], TT[:, 4 * g + h, :], idn)
                    last.then_inc(t1_psum, 1)
                pe.wait_ge(kv_nat, 4 * (c + 1))
                for s in range(1, LEVELS):
                    for g in range(2):
                        pe.wait_ge(atm_ready, 2 * LEVELS * c + 2 * s + g + 1)
                        if s == 1:
                            pe.wait_ge(p1_ready, 2 * LEVELS * c + g + 1)
                        else:
                            pe.wait_ge(t_ready, 2 * (LEVELS - 1) * c + 2 * (s - 2) + g + 1)
                        for h in range(4):
                            last = pe.matmul(heads(3 * g)[:, h, :], ATm[:, 4 * g + h, :], T[:, 4 * g + h, :],
                                             start=True, stop=True)
                        last.then_inc(p1_psum, 1)
                    for g in range(2):
                        pe.wait_ge(p1_ready, 2 * LEVELS * c + 2 * s + g + 1)
                        if s < LEVELS - 1:
                            for h in range(4):
                                pe.matmul(heads(3 * g + 1)[:, h, :], TT[:, 4 * g + h, :], P1[:, 4 * g + h, :],
                                          start=True, stop=True)
                        for h in range(4):
                            last = pe.matmul(heads(3 * g + 2)[:, h, :], P1[:, 4 * g + h, :], TT[:, 4 * g + h, :],
                                             start=True, stop=True)
                        last.then_inc(dd_psum, 1)
                pe.wait_ge(t_ready, 2 * (LEVELS - 1) * (c + 1))
                if c:
                    for h in range(HEADS):
                        last = pe.matmul(heads(h // 4)[:, h % 4, :], qkv[:, 8 + h, cs], S[:, h, :], start=True, stop=True)
                    last.then_inc(ks_psum, 1)
                pe.wait_ge(r_ready, c + 1)
                for h in range(HEADS):
                    last = pe.matmul(heads(2 + h // 4)[:, h % 4, :], TT[:, h, :], Vn[:, h, :], start=True, stop=True)
                last.then_inc(vn_psum, 1)
                pe.wait_ge(vn_ready, 2 * (c + 1))
                for h in range(HEADS):
                    out = heads(4 + h // 4)[:, h % 4, :]
                    if c:
                        pe.matmul(out, S[:, h, :], qkv[:, h, cs], start=True, stop=False)
                    pe.matmul(out, P1[:, h, :], DM[:, h, :], start=c == 0, stop=True)
                for h in range(HEADS):
                    last = pe.matmul(heads(6 + h // 4)[:, h % 4, :], Kn[:, h, :], P1[:, h, :], start=True, stop=True)
                last.then_inc(oS_psum, 1)
            pe.wait_ge(s_ready, 2 * NCH)
            for k in range(KT):
                pe.wait_ge(osq_ready, k + 1)
                pe.matmul(bank[k][:, 0:N], ones[:, :], osq[:, k, :], start=True, stop=True).then_inc(osq_psum, 1)
            pe.wait_ge(xh_ready, 16)
            pe.wait_ge(xl_ready, 16)
            for n in range(OUT0, GU0):
                if n >= OUT0 + 2:
                    pe.wait_ge(res_ready, 2 * (n - OUT0) - 2)
                dense_slot(pe, n, 2 * (n % 2), xh, xl)

            def layer_norm(l):
                for k in range(KT):
                    if l < 3:
                        pe.wait_ge(res_ready, 8 * l + k + 1)
                    last = pe.matmul(bank[4][:, 0:N], ones[:, :], xres[:, k, :], start=k == 0, stop=k == KT - 1)
                last.then_inc(mean_psum, 1)
                for k in range(KT):
                    pe.wait_ge(lnsq_ready, 8 * l + k + 1)
                    last = pe.matmul(bank[5][:, 0:N], ones[:, :], lnsq[:, k, :], start=k == 0, stop=k == KT - 1)
                last.then_inc(var_psum, 1)

            layer_norm(0)
            pe.wait_ge(xh_ready, 24)
            pe.wait_ge(xl_ready, 24)
            for i in range(FF // 256):
                if i >= 2:
                    pe.wait_ge(gate_silu, 2 * (i - 1))
                    pe.wait_ge(h_ready, 2 * (i - 1))
                dense_slot(pe, GU0 + 2 * i, 4 * (i % 2), xh, xl)
                dense_slot(pe, GU0 + 2 * i + 1, 4 * (i % 2) + 2, xh, xl)
            pe.wait_ge(hl_ready, FT)
            for n in range(DOWN0, SCI0):
                wh = high[:, n % SPLIT, :].rearrange("p (k f) -> p k f", k=2)
                wl = low[:, n % SPLIT, :].rearrange("p (k f) -> p k f", k=2)
                pe.wait_ge(high_ready, n + 1)
                f = 2 * (n - DOWN0)
                for d in range(KT):
                    ds = slice(128 * d, 128 * d + 128)
                    for k in range(2):
                        pe.matmul(bank[d][:, 0:N], wh[:, k, ds], hh[:, f + k, :], start=f + k == 0, stop=False)
                        pe.matmul(bank[d][:, 0:N], wh[:, k, ds], hl[:, f + k, :], start=False, stop=False)
                pe.wait_ge(low_ready, n + 1)
                for d in range(KT):
                    ds = slice(128 * d, 128 * d + 128)
                    for k in range(2):
                        last = pe.matmul(bank[d][:, 0:N], wl[:, k, ds], hh[:, f + k, :], start=False, stop=f + k == FT - 1)
                last.then_inc(slot_used, 1)
            pe.wait_ge(res_ready, 16)
            layer_norm(1)
            pe.wait_ge(xh_ready, 32)
            pe.wait_ge(xl_ready, 32)
            for i in range(D // 256):
                if i >= 2:
                    pe.wait_ge(c_copied, 2 * (i - 1))
                    pe.wait_ge(u_ready, 2 * (i - 1))
                dense_slot(pe, SCI0 + 2 * i, 4 * (i % 2), xh, xl)
                dense_slot(pe, SCI0 + 2 * i + 1, 4 * (i % 2) + 2, xh, xl)
            for i in range(D // 256):
                pe.wait_ge(c_copied, 6 if i < 2 else 8)
                pe.wait_ge(u_ready, 6 if i < 2 else 8)
                dense_slot(pe, SCI0 + 2 * D // 256 + i, 2 * i, xh, xl)
            pe.wait_ge(sy_ready, 8)
            for i in range(2):
                for t in range(4):
                    last = pe.transpose(bank[4 + i][0:10, 128 * t:128 * t + 128], su[:, 4 * i + t, NP:NP + 10], idn)
                last.then_inc(stail_psum, 1)
            pe.wait_ge(yl_ready, 8)
            for n in range(SCO0, MOE0):
                i = n - SCO0
                if i >= 2:
                    pe.wait_ge(res_ready, 16 + 2 * i - 2)
                dense_slot(pe, n, 2 * (i % 2), yh, yl)
            pe.wait_ge(stail_sb, 2)
            layer_norm(2)
            pe.wait_ge(x_new, 24)
            for i in range(6):
                tt, n_tok = i // 2, (128 if i < 4 else NS)
                for t in range(4):
                    last = pe.transpose(bank[i][0:n_tok, 128 * t:128 * t + 128],
                                        xres[:, 4 * (i % 2) + t, 128 * tt:128 * tt + n_tok], idn)
                last.then_inc(xn_psum, 1)
            for tt in range(3):
                n_tok = 128 if tt < 2 else NS
                for k in range(KT):
                    last = pe.matmul(bank[6][0:n_tok, 8 * tt:8 * tt + 8], xres[:, k, 128 * tt:128 * tt + n_tok], wr[:, k, :],
                                     start=k == 0, stop=k == KT - 1)
            last.then_inc(logit_psum, 1)
            pe.wait_ge(sel_ready, 1)
            for tt in range(4):
                for s in range(min(tt + 1, 3)):
                    last = pe.matmul(bank[7][:, 8 * tt:8 * tt + 8], upper[:, :] if s == tt else ones[:, :], sel[:, s, :],
                                     start=s == 0, stop=s == min(tt, 2))
            last.then_inc(rank_psum, 1)

            def gather(jobs):
                pe.wait_ge(pick_ready, jobs + 1)
                for b, src in ((0, xnh), (2, xnl)):
                    for g in range(2):
                        for d in range(4):
                            ds = slice(512 * g + 128 * d, 512 * g + 128 * d + 128)
                            for tt in range(3):
                                last = pe.matmul(heads(b + g)[:, d, :], src[:, tt, ds], pick[:, tt, :], start=tt == 0, stop=tt == 2)
                        last.then_inc(xg_psum, 1)

            pe.wait_ge(xnh_ready, 6)
            pe.wait_ge(xnl_ready, 6)
            gather(0)
            pe.wait_ge(tiles_ready, 1)
            tiles = pe.value_load(tiles_i[0:1, 0:1], min_val=1, max_val=TILES)
            with pe.Fori(0, tiles) as t:
                with pe.Fori(0, EX) as e:
                    job = t * EX + e
                    done, units = job * EXPERT_SLOTS, job * UNITS

                    def gate_or_up(u, w):
                        out = bank[2 * (u % 2) + w][:, :]
                        if u >= 2:
                            pe.wait_ge(sgx_ready if w == 0 else hx_ready, units + (u - 1))
                        for kh in range(2):
                            n = MOE0 + unit_first(u) + 2 * w + kh
                            wh = high[:, n % SPLIT, :].rearrange("p (k f) -> p k f", k=4)
                            wl = low[:, n % SPLIT, :].rearrange("p (k f) -> p k f", k=4)
                            pe.wait_ge(high_ready, done + (n + 1))
                            for k in range(4):
                                pe.matmul(out, xgh[:, 4 * kh + k, :], wh[:, k, :], start=kh + k == 0, stop=False)
                                pe.matmul(out, xgl[:, 4 * kh + k, :], wh[:, k, :], start=False, stop=False)
                            pe.wait_ge(low_ready, done + (n + 1))
                            for k in range(4):
                                last = pe.matmul(out, xgh[:, 4 * kh + k, :], wl[:, k, :], start=False, stop=kh == 1 and k == 3)
                            last.then_inc(slot_used, 1)

                    def transpose_hidden(u):
                        pe.wait_ge(hx_ready, units + (u + 1))
                        if u:
                            pe.wait_ge(htl_ready, units + u)
                        for q in range(4):
                            last = pe.transpose(bank[6][:, 128 * q:128 * q + 128], hx[:, u % 2, 128 * q:128 * q + 128], idn)
                        last.then_inc(ht_psum, 1)

                    def down(u):
                        pe.wait_ge(hth_ready, units + (u + 1))
                        pe.wait_ge(htl_ready, units + (u + 1))
                        for kh in range(2):
                            n = MOE0 + down_first(u) + kh
                            wh = high[:, n % SPLIT, :].rearrange("p (k f) -> p k f", k=2)
                            wl = low[:, n % SPLIT, :].rearrange("p (k f) -> p k f", k=2)
                            pe.wait_ge(high_ready, done + (n + 1))
                            for k in range(2):
                                hs = slice(256 * kh + 128 * k, 256 * kh + 128 * k + 128)
                                for src in (hth, htl):
                                    for g in range(2):
                                        pe.matmul(bank[4 + g][:, :], src[:, u % 2, hs], wh[:, k, 512 * g:512 * g + 512],
                                                  start=u + kh + k == 0 and src is hth, stop=False)
                            pe.wait_ge(low_ready, done + (n + 1))
                            for k in range(2):
                                hs = slice(256 * kh + 128 * k, 256 * kh + 128 * k + 128)
                                for g in range(2):
                                    last = pe.matmul(bank[4 + g][:, :], hth[:, u % 2, hs], wl[:, k, 512 * g:512 * g + 512],
                                                     start=False, stop=u == UNITS - 1 and kh + k == 2)
                            last.then_inc(slot_used, 1)

                    pe.wait_ge(xgh_ready, job * 2 + 2)
                    pe.wait_ge(xgl_ready, job * 2 + 2)
                    for u in range(UNITS):
                        gate_or_up(u, 0)
                        if u:
                            transpose_hidden(u - 1)
                        gate_or_up(u, 1)
                        if u:
                            down(u - 1)
                        else:
                            pe.wait_ge(pickg_ready, job + 1)
                            pe.wait_ge(scat_done, job * KT + 1)
                            for tt in range(3):
                                n_tok = 128 if tt < 2 else NS
                                last = pe.transpose(bank[7][:, 128 * tt:128 * tt + n_tok], pickg[:, tt, :], idn) if tt < 2 else \
                                    pe.matmul(bank[7][:, NP:N], pickg[:, 2, :], ident[:, 0:NS], start=True, stop=True)
                            last.then_inc(pt_psum, 1)
                    transpose_hidden(UNITS - 1)
                    gather(job + 1)
                    down(UNITS - 1)
                    for ready in (yxh_ready, yxl_ready):
                        pe.wait_ge(ready, job * 2 + 2)
                    for ready in (pth_ready, ptl_ready):
                        pe.wait_ge(ready, job + 1)
                    for d in range(KT):
                        if d >= 2:
                            pe.wait_ge(scat_done, job * KT + d)
                        ds = slice(128 * d, 128 * d + 128)
                        out = bank[6 + d % 2][:, 0:N]
                        pe.matmul(out, yxh[:, ds], pth[:, :], start=True, stop=False)
                        pe.matmul(out, yxl[:, ds], pth[:, :], start=False, stop=False)
                        pe.matmul(out, yxh[:, ds], ptl[:, :], start=False, stop=True).then_inc(scat_psum, 1)
            pe.wait_ge(scat_done, tiles * (EX * KT) + 1)
            layer_norm(3)
            pe.wait_ge(x_new, 32)
            for i in range(6):
                tt, n_tok = i // 2, (128 if i < 4 else NS)
                for q in range(4):
                    last = pe.transpose(bank[i][0:n_tok, 128 * q:128 * q + 128],
                                        xres[:, 4 * (i % 2) + q, 128 * tt:128 * tt + n_tok], idn)
                last.then_inc(y_psum, 1)


_INS = ['x_prompt', 'x_sample', 'state_gdn_S', 'state_gdn_conv', 'state_sconv', 'ln_g', 'ln_b', 'gdn_w_in',
        'gdn_conv_w', 'gdn_a_log', 'gdn_dt_bias', 'gdn_norm_w', 'gdn_w_out', 'sc_w_in', 'sc_conv_w', 'sc_w_out',
        'ffn_w_gu', 'ffn_w_down', 'moe_w_router', 'moe_w_gu', 'moe_w_down']
_OUTS = [(1, 256, 1024), (8, 1, 1024), (1, 1, 8, 128, 128), (1, 8, 8, 128, 128), (1, 1, 3, 3072), (1, 8, 3, 3072),
         (1, 1, 2, 1024), (1, 8, 2, 1024)]


def kernel(**inputs):
    import numpy as _np
    import concourse.bacc as _bacc
    from concourse import mybir as _mybir
    from concourse.bass_utils import run_bass_kernel_spmd as _run

    nc = _bacc.Bacc("TRN2", target_bir_lowering=False, num_devices=1)
    arrays, args = {}, []
    for name in _INS:
        a = _np.ascontiguousarray(inputs[name])
        arrays[f"in_{name}_dram"] = a
        args.append(nc.dram_tensor(f"in_{name}_dram", a.shape, _mybir.dt.from_np(a.dtype), kind="ExternalInput").ap())
    for i, shape in enumerate(_OUTS):
        args.append(nc.dram_tensor(f"out_{i}_dram", shape, _mybir.dt.float32, kind="ExternalOutput").ap())
    hybrid_step(nc, *args)
    r = _run(nc, [arrays], core_ids=[0])
    return tuple(r.results[0][f"out_{i}_dram"] for i in range(len(_OUTS)))
```
